# Optimizing a Trainium2 kernel written in Bass

```python
import math
import jax, jax.numpy as jnp
from jax import lax
import numpy as np

D_MODEL = 1024
BATCH = 1
SEQ = 256
DEPTH = 2
DEC_BATCH = 8
DEC_SEQ = 4
PAST_LEN = 2048
PAGE_SIZE = 128

GLA_HEADS = 4
GLA_DK = 64
GLA_DV = 128
GLA_RANK = 16
GLA_TAU = 16.0
GLA_CHUNK = 64
GMLP_GROUPS = 4
GMLP_WIDTH = 512
GMLP_CHUNK = 128
CONV_WIDTH = 512
CONV_K = 31
SWA_HEADS = 8
SWA_KV_HEADS = 2
SWA_GROUP = SWA_HEADS // SWA_KV_HEADS
SWA_HEAD_DIM = 64
WINDOW = 128
ROPE_DIM = SWA_HEAD_DIM // 4
ROPE_THETA = 500000.0
N_BRANCH = 4
BRANCH_WIDTH = 512
FFN_HIDDEN = ((8 * D_MODEL // 3 + 255) // 256) * 256
IN_SPLITS = (GLA_HEADS * GLA_DK, GLA_HEADS * GLA_DK, GLA_HEADS * GLA_DV, GLA_HEADS * GLA_DV, GLA_RANK,
             GMLP_WIDTH, GMLP_WIDTH, CONV_WIDTH, CONV_WIDTH,
             SWA_HEADS * SWA_HEAD_DIM, SWA_KV_HEADS * SWA_HEAD_DIM, SWA_KV_HEADS * SWA_HEAD_DIM)
IN_COLS = sum(IN_SPLITS)
NORM_EPS = 1e-6
LN_EPS = 1e-5

kernel_name = "hybrid_gla_gmlp_conv_swa_step"

def rmsnorm(x, g):
    xf = x.astype(jnp.float32)
    y = xf * lax.rsqrt(jnp.mean(xf * xf, axis=-1, keepdims=True) + NORM_EPS)
    return (y * g.astype(jnp.float32)).astype(x.dtype)

def layernorm(x, g, b):
    xf = x.astype(jnp.float32)
    mu = jnp.mean(xf, axis=-1, keepdims=True)
    xc = xf - mu
    var = jnp.mean(xc * xc, axis=-1, keepdims=True)
    return (xc * lax.rsqrt(var + LN_EPS) * g.astype(jnp.float32) + b.astype(jnp.float32)).astype(x.dtype)

def split_cols(z):
    idx = [int(i) for i in np.cumsum(IN_SPLITS)[:-1]]
    return jnp.split(z, idx, axis=-1)

def gla_recurrence(q, k, v, log_a, s0):
    B, L, H, _ = q.shape
    c = math.gcd(L, GLA_CHUNK)
    n = L // c

    def blocks(t):
        return t.astype(jnp.float32).reshape(B, n, c, H, t.shape[-1]).transpose(1, 0, 3, 2, 4)

    causal = jnp.tril(jnp.ones((c, c), dtype=bool))

    def step(s, inp):
        qc, kc, vc, ac = inp
        bcum = lax.cumsum(ac, axis=2)
        q_in = qc * jnp.exp(bcum)
        att = jnp.einsum('bhid,bhjd->bhij', q_in, kc * jnp.exp(-bcum))
        att = jnp.where(causal, att, 0.0)
        o = jnp.einsum('bhij,bhjv->bhiv', att, vc) + jnp.einsum('bhid,bhdv->bhiv', q_in, s)
        b_last = bcum[:, :, -1:, :]
        s_new = jnp.exp(b_last[:, :, 0, :])[..., None] * s + jnp.einsum(
            'bhjd,bhjv->bhdv', kc * jnp.exp(b_last - bcum), vc)
        return s_new, o

    s_fin, ob = lax.scan(step, s0.astype(jnp.float32), (blocks(q), blocks(k), blocks(v), blocks(log_a)))
    o = ob.transpose(1, 0, 3, 2, 4).reshape(B, L, H, v.shape[-1])
    return o, s_fin

def gmlp_spatial(v, w_s, b_s):
    B, L, _ = v.shape
    n = -(-L // GMLP_CHUNK)
    pad = n * GMLP_CHUNK - L
    vp = jnp.pad(v, ((0, 0), (0, pad), (0, 0))).reshape(
        B, n, GMLP_CHUNK, GMLP_GROUPS, GMLP_WIDTH // GMLP_GROUPS)
    w = jnp.where(jnp.tril(jnp.ones((GMLP_CHUNK, GMLP_CHUNK), dtype=bool)), w_s, 0.0)
    s = jnp.einsum('gts,bnsgc->bntgc', w, vp) + b_s.T[None, None, :, :, None]
    return s.reshape(B, n * GMLP_CHUNK, GMLP_WIDTH)[:, :L]

def causal_depthwise_conv(h_ext, w, b):
    C = h_ext.shape[-1]
    y = lax.conv_general_dilated(h_ext, w[:, None, :].astype(h_ext.dtype), window_strides=(1,),
                                 padding='VALID', dimension_numbers=('NWC', 'WIO', 'NWC'),
                                 feature_group_count=C)
    return y + b

def rope_partial(x, pos):
    half = ROPE_DIM // 2
    inv = jnp.exp(-math.log(ROPE_THETA) * jnp.arange(half, dtype=jnp.float32) * (2.0 / ROPE_DIM))
    ang = pos.astype(jnp.float32)[:, None] * inv[None, :]
    cos = jnp.cos(ang)[:, None, :]
    sin = jnp.sin(ang)[:, None, :]
    xf = x.astype(jnp.float32)
    x1 = xf[..., :half]
    x2 = xf[..., half:ROPE_DIM]
    out = jnp.concatenate([x1 * cos - x2 * sin, x2 * cos + x1 * sin, xf[..., ROPE_DIM:]], axis=-1)
    return out.astype(x.dtype)

def sink_attention(q, k, v, mask, sinks):
    s = jnp.einsum('...qhgd,...shd->...hgqs', q, k, preferred_element_type=jnp.float32) * (SWA_HEAD_DIM ** -0.5)
    s = jnp.where(mask[..., None, None, :, :], s, -jnp.inf)
    sink = sinks.astype(jnp.float32)[:, :, None, None]
    m = jnp.maximum(jnp.max(s, axis=-1, keepdims=True), sink)
    p = jnp.exp(s - m)
    denom = jnp.sum(p, axis=-1, keepdims=True) + jnp.exp(sink - m)
    return jnp.einsum('...hgqs,...shd->...qhgd', (p / denom).astype(v.dtype), v)

def swa_prompt(qg, k, v, sinks):
    B, L = qg.shape[:2]
    n = L // WINDOW
    qb = qg.reshape(B, n, WINDOW, SWA_KV_HEADS, SWA_GROUP, SWA_HEAD_DIM)
    kb = k.reshape(B, n, WINDOW, SWA_KV_HEADS, SWA_HEAD_DIM)
    vb = v.reshape(B, n, WINDOW, SWA_KV_HEADS, SWA_HEAD_DIM)
    shift = ((0, 0), (1, 0), (0, 0), (0, 0), (0, 0))
    kk = jnp.concatenate([jnp.pad(kb, shift)[:, :-1], kb], axis=2)
    vv = jnp.concatenate([jnp.pad(vb, shift)[:, :-1], vb], axis=2)
    blk = jnp.arange(n)[:, None]
    qpos = blk * WINDOW + jnp.arange(WINDOW)[None, :]
    kpos = (blk - 1) * WINDOW + jnp.arange(2 * WINDOW)[None, :]
    d = qpos[:, :, None] - kpos[:, None, :]
    mask = (d >= 0) & (d < WINDOW) & (kpos[:, None, :] >= 0)
    o = sink_attention(qb, kk, vv, mask, sinks)
    return o.reshape(B, L, SWA_HEADS * SWA_HEAD_DIM), k[:, -WINDOW:], v[:, -WINDOW:]

def swa_sample(qg, k, v, k_hist, v_hist, sinks):
    B, Lq = qg.shape[:2]
    kk = jnp.concatenate([k_hist.astype(k.dtype), k], axis=1)
    vv = jnp.concatenate([v_hist.astype(v.dtype), v], axis=1)
    qpos = PAST_LEN + jnp.arange(Lq)
    kpos = PAST_LEN - WINDOW + jnp.arange(WINDOW + Lq)
    d = qpos[:, None] - kpos[None, :]
    mask = (d >= 0) & (d < WINDOW)
    o = sink_attention(qg, kk, vv, mask, sinks)
    return o.reshape(B, Lq, SWA_HEADS * SWA_HEAD_DIM), kk[:, -WINDOW:], vv[:, -WINDOW:]

def trunk_layer(x, pos0, gla_s0, conv_hist, k_hist, v_hist, prompt, p):
    (norm1_g, w_in, b_in, w_alpha2, b_alpha, gla_norm_g, gmlp_ln_g, gmlp_ln_b, w_spatial, b_spatial,
     conv_w, conv_b, conv_ln_g, conv_ln_b, q_norm_g, k_norm_g, sinks, w_gate, b_gate, w_branch,
     w_out, norm2_g, w_gate_up, w_down) = p
    B, L, _ = x.shape
    xn = rmsnorm(x, norm1_g)
    z = xn @ w_in + b_in
    a_q, a_k, a_v, a_r, a_lr, b_u, b_v, c_a, c_g, d_q, d_k, d_v = split_cols(z)

    q = a_q.reshape(B, L, GLA_HEADS, GLA_DK) * (GLA_DK ** -0.5)
    k = a_k.reshape(B, L, GLA_HEADS, GLA_DK)
    v = a_v.reshape(B, L, GLA_HEADS, GLA_DV)
    log_a = jax.nn.log_sigmoid((a_lr @ w_alpha2 + b_alpha).astype(jnp.float32)).reshape(
        B, L, GLA_HEADS, GLA_DK) / GLA_TAU
    o_gla, gla_new = gla_recurrence(q, k, v, log_a, gla_s0)
    o_a = rmsnorm(o_gla.astype(x.dtype), gla_norm_g).reshape(B, L, GLA_HEADS * GLA_DV) * jax.nn.silu(a_r)

    u = jax.nn.gelu(b_u, approximate=False)
    gv = layernorm(jax.nn.gelu(b_v, approximate=False), gmlp_ln_g, gmlp_ln_b)
    o_b = u * gmlp_spatial(gv, w_spatial, b_spatial)

    h = c_a * jax.nn.sigmoid(c_g)
    h_ext = jnp.concatenate([conv_hist.astype(h.dtype), h], axis=1)
    o_c = jax.nn.silu(layernorm(causal_depthwise_conv(h_ext, conv_w, conv_b), conv_ln_g, conv_ln_b))
    conv_new = h_ext[:, -(CONV_K - 1):]

    pos = pos0 + jnp.arange(L)
    qd = rope_partial(rmsnorm(d_q.reshape(B, L, SWA_HEADS, SWA_HEAD_DIM), q_norm_g), pos)
    kd = rope_partial(rmsnorm(d_k.reshape(B, L, SWA_KV_HEADS, SWA_HEAD_DIM), k_norm_g), pos)
    vd = d_v.reshape(B, L, SWA_KV_HEADS, SWA_HEAD_DIM)
    qg = qd.reshape(B, L, SWA_KV_HEADS, SWA_GROUP, SWA_HEAD_DIM)
    sk = sinks.reshape(SWA_KV_HEADS, SWA_GROUP)
    if prompt:
        o_d, k_new, v_new = swa_prompt(qg, kd, vd, sk)
    else:
        o_d, k_new, v_new = swa_sample(qg, kd, vd, k_hist, v_hist, sk)

    gates = jax.nn.sigmoid(xn @ w_gate + b_gate).reshape(B, L, N_BRANCH, D_MODEL)
    merged = 0.0
    for i, o_br in enumerate((o_a, o_b, o_c, o_d)):
        merged = merged + gates[:, :, i] * (o_br @ w_branch[i])
    x = x + merged @ w_out

    g, up = jnp.split(rmsnorm(x, norm2_g) @ w_gate_up, 2, axis=-1)
    x = x + (jax.nn.silu(g) * up) @ w_down
    return x, gla_new, conv_new, k_new, v_new, gv

def setup_inputs(seed: int = 0) -> dict:
    key = jax.random.key(seed)
    counter = [0]

    def nrm(shape, scale):
        counter[0] += 1
        return jax.random.normal(jax.random.fold_in(key, counter[0]), shape, jnp.float32) * scale

    def gain(shape):
        return 1.0 + nrm(shape, 0.05)

    Dp = DEPTH
    return {
        "x_prompt": nrm((BATCH, SEQ, D_MODEL), 1.0),
        "x_sample": nrm((DEC_BATCH, DEC_SEQ, D_MODEL), 1.0),
        "state_gla": nrm((Dp, DEC_BATCH, GLA_HEADS, GLA_DK, GLA_DV), 1.0),
        "state_conv": nrm((Dp, DEC_BATCH, CONV_K - 1, CONV_WIDTH), 0.5),
        "cache_swa_k": nrm((Dp, DEC_BATCH, WINDOW, SWA_KV_HEADS, SWA_HEAD_DIM), 1.0),
        "cache_swa_v": nrm((Dp, DEC_BATCH, WINDOW, SWA_KV_HEADS, SWA_HEAD_DIM), 1.0),
        "norm1_g": gain((Dp, D_MODEL)),
        "w_in": nrm((Dp, D_MODEL, IN_COLS), D_MODEL ** -0.5),
        "b_in": nrm((Dp, IN_COLS), 0.02),
        "w_alpha2": nrm((Dp, GLA_RANK, GLA_HEADS * GLA_DK), GLA_RANK ** -0.5),
        "b_alpha": nrm((Dp, GLA_HEADS * GLA_DK), 0.1),
        "gla_norm_g": gain((Dp, GLA_DV)),
        "gmlp_ln_g": gain((Dp, GMLP_WIDTH)),
        "gmlp_ln_b": nrm((Dp, GMLP_WIDTH), 0.02),
        "w_spatial": nrm((Dp, GMLP_GROUPS, GMLP_CHUNK, GMLP_CHUNK), 0.5 * GMLP_CHUNK ** -0.5),
        "b_spatial": gain((Dp, GMLP_GROUPS, GMLP_CHUNK)),
        "conv_w": nrm((Dp, CONV_K, CONV_WIDTH), CONV_K ** -0.5),
        "conv_b": nrm((Dp, CONV_WIDTH), 0.02),
        "conv_ln_g": gain((Dp, CONV_WIDTH)),
        "conv_ln_b": nrm((Dp, CONV_WIDTH), 0.02),
        "q_norm_g": gain((Dp, SWA_HEAD_DIM)),
        "k_norm_g": gain((Dp, SWA_HEAD_DIM)),
        "sinks": nrm((Dp, SWA_HEADS), 0.5),
        "w_gate": nrm((Dp, D_MODEL, N_BRANCH * D_MODEL), D_MODEL ** -0.5),
        "b_gate": nrm((Dp, N_BRANCH * D_MODEL), 0.02),
        "w_branch": nrm((Dp, N_BRANCH, BRANCH_WIDTH, D_MODEL), BRANCH_WIDTH ** -0.5),
        "w_out": nrm((Dp, D_MODEL, D_MODEL), 0.5 * D_MODEL ** -0.5),
        "norm2_g": gain((Dp, D_MODEL)),
        "w_gate_up": nrm((Dp, D_MODEL, 2 * FFN_HIDDEN), D_MODEL ** -0.5),
        "w_down": nrm((Dp, FFN_HIDDEN, D_MODEL), 0.5 * FFN_HIDDEN ** -0.5),
    }

def reference(x_prompt, x_sample, state_gla, state_conv, cache_swa_k, cache_swa_v,
              norm1_g, w_in, b_in, w_alpha2, b_alpha, gla_norm_g, gmlp_ln_g, gmlp_ln_b,
              w_spatial, b_spatial, conv_w, conv_b, conv_ln_g, conv_ln_b, q_norm_g, k_norm_g,
              sinks, w_gate, b_gate, w_branch, w_out, norm2_g, w_gate_up, w_down):
    yp, ys = x_prompt, x_sample
    bp = x_prompt.shape[0]
    gla_p, gla_s, conv_p, conv_s, kp, vp, ks, vs, gm_s = [], [], [], [], [], [], [], [], []
    for l in range(DEPTH):
        prm = (norm1_g[l], w_in[l], b_in[l], w_alpha2[l], b_alpha[l], gla_norm_g[l], gmlp_ln_g[l],
               gmlp_ln_b[l], w_spatial[l], b_spatial[l], conv_w[l], conv_b[l], conv_ln_g[l],
               conv_ln_b[l], q_norm_g[l], k_norm_g[l], sinks[l], w_gate[l], b_gate[l], w_branch[l],
               w_out[l], norm2_g[l], w_gate_up[l], w_down[l])
        gla0 = jnp.zeros((bp, GLA_HEADS, GLA_DK, GLA_DV), jnp.float32)
        conv0 = jnp.zeros((bp, CONV_K - 1, CONV_WIDTH), yp.dtype)
        yp, g1, c1, k1, v1, _ = trunk_layer(yp, 0, gla0, conv0, None, None, True, prm)
        ys, g2, c2, k2, v2, gv2 = trunk_layer(ys, PAST_LEN, state_gla[l], state_conv[l],
                                              cache_swa_k[l], cache_swa_v[l], False, prm)
        gla_p.append(g1); conv_p.append(c1); kp.append(k1); vp.append(v1)
        gla_s.append(g2); conv_s.append(c2); ks.append(k2); vs.append(v2); gm_s.append(gv2)
    new_gla_prompt = jnp.stack(gla_p, 0)
    new_gla_sample = jnp.stack(gla_s, 0)
    new_conv_prompt = jnp.stack(conv_p, 0)
    new_conv_sample = jnp.stack(conv_s, 0)
    new_k_prompt = jnp.stack(kp, 0)
    new_v_prompt = jnp.stack(vp, 0)
    new_k_sample = jnp.stack(ks, 0)
    new_v_sample = jnp.stack(vs, 0)
    new_gmlp_v_sample = jnp.stack(gm_s, 0)
    return (yp, ys, new_gla_prompt, new_gla_sample, new_conv_prompt, new_conv_sample,
            new_k_prompt, new_v_prompt, new_k_sample, new_v_sample, new_gmlp_v_sample)


_drawn_inputs = setup_inputs


def setup_inputs(seed=0):
    import zlib

    import numpy as np

    out = dict(_drawn_inputs(seed))
    spreads = {}
    factors = {'gla_norm_g': 5.172,
     'gmlp_ln_b': 2.879,
     'b_spatial': 4.407,
     'conv_b': 5.787,
     'conv_ln_g': 3.907,
     'conv_ln_b': 8.0,
     'q_norm_g': 8.0,
     'sinks': 55.774,
     'b_gate': 8.0,
     'norm2_g': 2.98}
    for name, (base, spread) in spreads.items():
        noise = np.random.default_rng([zlib.crc32(name.encode()), seed]).standard_normal(out[name].shape)
        drawn = base * np.exp(spread * noise) if base else spread * noise
        out[name] = __import__('jax').numpy.asarray(drawn.astype(out[name].dtype))
    for name, factor in factors.items():
        out[name] = (out[name] * factor).astype(out[name].dtype)
    return out
```

```python
import math
from contextlib import ExitStack

import concourse.bass as bass
import numpy as np
from concourse import mybir

DEPTH, D_MODEL, SEQ, DEC_B, DEC_T, PAST = 2, 1024, 256, 8, 4, 2048
WIN, HD, CONV_K, CONV_W = 128, 64, 31, 512
FFN = 2816
IN_COLS = 4368
P = 128
TS = DEC_B * DEC_T
T = SEQ + TS
KC = D_MODEL // P
HC = FFN // P
NSEG = SEQ // 64
HIST = CONV_K - 1
EXT = DEC_T + HIST
NEG = -1.0e30

C_A, C_G, D_Q, D_K, D_V, A_Q, A_K, A_V, A_R, B_U, B_V = 0, 4, 8, 12, 13, 14, 16, 18, 22, 26, 30
NZ = 34
HALVED = (D_K, D_V)

RING = 4
UNIT = P
SLOT = KC * UNIT
DOWN_UNITS = (6, 8, 8)
Z0 = 0
G0 = Z0 + NZ + len(HALVED)
BR0 = G0 + 4 * KC
O0 = BR0 + 2 * KC
U0 = O0 + KC
DN0 = U0 + 2 * HC
BLOCKS = DN0 + 3 * KC
TZ, TG = 0, NZ
TB = TG + 4 * KC
TO = TB + 4 * KC
TU = TO + KC
TD = TU + 2 * HC
TILES = TD + KC
PER_BANK = TILES // 2
POOL_BLOCKS = BR0
DVE_BLOCKS = BLOCKS - POOL_BLOCKS
assert BLOCKS % RING == 0 and G0 % RING == 0 and U0 % RING == 0 and DN0 % RING == 0 and TILES % 2 == 0

_cols, PARAM_AT = 0, {}
for _name, _n in (("b_in", NZ), ("b_gate", 4 * KC), ("norm1", KC), ("norm2", KC), ("b_alpha", 2), ("gla_g", 1),
                  ("gmlp_g", 4), ("gmlp_b", 4), ("conv_w", 4 * CONV_K), ("conv_b", 4), ("conv_g", 4),
                  ("conv_lb", 4), ("q_g", 1), ("k_g", 1), ("sink", 18), ("b_lr", 1)):
    PARAM_AT[_name] = _cols
    _cols += _n
PARAMS = _cols
CONST_AT, _cols = {}, 0
for _name, _n in (("ones", P), ("heads", P), ("turn", P), ("ident", P), ("upper", P), ("band", 2 * P),
                  ("own", DEC_B), ("later", P), ("new", TS), ("seg", T), ("cos", T), ("sin", T),
                  ("gla", 64), ("gla_s", TS), ("of_b", DEC_B), ("rep", TS)):
    CONST_AT[_name] = _cols
    _cols += _n
CONSTS = _cols

STEP = dict(
    c_gate=9, qk_sq=15, qk_sums=16, qk_rstd=17, qk_turned=19, scores0=21, tok_copied=21, scores1=22, exp0=24,
    probs_turned=28, probs_copied=28, prompt_pv=30, prompt_od=30, smp_new=31, exp_s=33, probs_s_turned=36,
    gelu=36, probs_s_copied=36, smp_pv=38, smp_od=38, decay_in=39, decay_log=39, decay_exp=41, att_in=44,
    k_copied=44, chunks=46, smp_out=48, gla_o=49, smp_update=50, gla_sums=53, gla_rstd=54, gm_mean=55, gm_sq=56,
    gm_var=57, gv_done=58, gv_turned=60, gv_copied=60, mixed=62, cv_mean=64, cv_sq=65, cv_var=66, c_out=67)

CONV_AHEAD, CONV_BETWEEN = 10, 2
DVE_LINKS = 161
ACT_LINKS = 3
STORES_PER_LAYER = 9


def z_blocks():
    for t in range(NZ):
        if t in HALVED:
            yield t, 0, 4
            yield t, 4, 4
        else:
            yield t, 0, 8


def trunk_program(nc, dram):
    f32, f32r = mybir.dt.float32, mybir.dt.float32r
    ACT, ALU, AX = mybir.ActivationFunctionType, mybir.AluOpType, mybir.AxisListType
    ctx = ExitStack()
    with ctx:
        def sb(name, cols, dt=f32):
            return ctx.enter_context(nc.sbuf_tensor(name, [P, *cols], dt))

        def sem(name):
            return ctx.enter_context(nc.semaphore(name))

        over_at = -(-nc.sbuf_base // 32) * 32
        sb("over", [(NZ + 4 * KC) * T + 8])
        zg = nc.alloc_sbuf_tensor_at("zg", [P, NZ + 4 * KC, T], f32, offset=over_at)
        h_hi = nc.alloc_sbuf_tensor_at("h_hi", [P, HC, T], f32r, offset=over_at)
        h_lo = nc.alloc_sbuf_tensor_at("h_lo", [P, HC, T], f32r, offset=over_at + 4 * HC * T)

        raw = sb("raw", [RING, SLOT])
        w_hi, w_lo = sb("w_hi", [RING, SLOT], f32r), sb("w_lo", [RING, SLOT], f32r)
        x = sb("x", [KC, T])
        x_hi, x_lo = sb("x_hi", [KC, T], f32r), sb("x_lo", [KC, T], f32r)
        z, gate = zg[:, 0:NZ, :], zg[:, NZ:NZ + 4 * KC, :]
        work = sb("work", [6144])
        kv = sb("kv", [2048])
        prm = sb("prm", [PARAMS])
        cst = sb("cst", [CONSTS])
        w_lr = sb("w_lr", [KC, 16])
        w_a2 = sb("w_a2", [2 * P])
        w_sp = sb("w_sp", [4, P])
        b_sp = sb("b_sp", [4, P])
        w_bd = sb("w_bd", [4, TS])
        hist_p = sb("hist_p", [4, SEQ + HIST])
        hist_s = sb("hist_s", [4, DEC_B, EXT])
        qz = sb("qz", [4, T])
        attz = sb("attz", [4, 2, P])
        vt = sb("vt", [2, P])
        vs = sb("vs", [2, P])
        small = sb("small", [5, 18])
        rs = sb("rs", [T])
        lr = sb("lr", [T])
        q_smp = sb("q_smp", [P])
        state = sb("state", [2, P])
        ps = ctx.enter_context(nc.psum_tensor("ps", [P, 8, 512], f32))

        def p(name, i=0, n=1):
            at = PARAM_AT[name] + i
            return prm[:, at:at + n]

        def c(name, n=None, i=0):
            at = CONST_AT[name] + i
            return cst[:, at:at + (n or P)]

        xn = work[:, 0:KC * T].rearrange("p (c t) -> p c t", t=T)
        sq5 = work[:, 0:5 * T].rearrange("p (c t) -> p c t", t=T)
        r5 = work[:, 5 * T:10 * T].rearrange("p (c t) -> p c t", t=T)
        prob = work[:, 0:3072]
        prob_t = work[:, 3072:6144]
        prob0 = prob[:, 0:1024].rearrange("p (h k) -> p h k", k=P)
        prob1 = prob[:, 1024:3072].rearrange("p (h k) -> p h k", k=2 * P)
        prob_s = prob[:, 0:2 * 1056].rearrange("p (v k) -> p v k", k=1056)
        prob0_t = prob_t[:, 0:1024]
        prob1_t = prob_t[:, 1024:3072].rearrange("p (a n) -> p a n", a=2)
        prob_st = prob_t[:, 0:2048].rearrange("p (v b r) -> p v b r", v=2, b=DEC_B)
        prob_nt = prob_t[:, 2048:2048 + 2 * P].rearrange("p (v r) -> p v r", v=2)
        gl = work[:, 0:2304].rearrange("p (a c t) -> p a c t", a=4, t=T)
        bcum, e_pos, k_neg, e_last = gl[:, 0], gl[:, 1], gl[:, 2], gl[:, 3]
        v_tok = zg[:, C_G:C_G + 4, :].rearrange("p a t -> p (a t)")[:, 0:1024]\
            .rearrange("p (a n) -> p a n", a=2)
        v_tok_s = work[:, 2304:2816]
        k_tok = work[:, 2816:3328].rearrange("p (a n) -> p a n", a=2)
        k_tok_s = work[:, 3328:3584]
        att_s = work[:, 3584:3712].rearrange("p (h i) -> p h i", h=4)
        k_own = work[:, 3712:5760].rearrange("p (b n) -> p b n", b=DEC_B)
        gla_o = z[:, A_Q:A_Q + 4, :]
        g_sq = work[:, 0:4 * T].rearrange("p (c t) -> p c t", t=T)
        g_tmp = work[:, 4 * T:8 * T].rearrange("p (c t) -> p c t", t=T)
        gv_tok = work[:, 2304:3328].rearrange("p (a n) -> p a n", a=2)
        gv_tok_s = work[:, 3328:3840]
        window = work[:, 3072:3072 + TS * CONV_K]
        gate_s = work[:, 2304:2304 + 2 * T].rearrange("p (a t) -> p a t", a=2)
        hidden = work[:, 2304 + 2 * T:2304 + 4 * T].rearrange("p (a t) -> p a t", a=2)
        def taps_of(k):
            a = hist_s[:, k, :, 0:DEC_T]
            return bass.AP(tensor=a.tensor, offset=a.offset, ap=[*a.ap, [1, CONV_K]])

        k_hist, v_hist = kv[:, 0:1024], kv[:, 1024:2048].rearrange("p (b n) -> p b n", b=DEC_B)
        s_smp = kv[:, :].rearrange("p (b a v) -> p b a v", b=DEC_B, a=2)

        raw_in = [sem(f"raw_in{s}") for s in range(RING)]
        hi_done = sem("hi_done")
        lo_pool = sem("lo_pool")
        lo_dve = sem("lo_dve")
        blocks_done = sem("blocks_done")
        bank_free = [sem(f"bank_free{i}") for i in range(2)]
        xh_done, xl_done = sem("xh_done"), sem("xl_done")
        xn_done = sem("xn_done")
        hid_hi, hid_lo, hid_free = sem("hid_hi"), sem("hid_lo"), sem("hid_free")
        summed = sem("summed")
        dve_link, act_link = sem("dve_link"), sem("act_link")
        x_in, const_in, prm_in, hist_in, kv_in, state_in = (
            sem(n) for n in ("x_in", "const_in", "prm_in", "hist_in", "kv_in", "state_in"))
        zeroed = sem("zeroed")
        stored = sem("stored")
        cached = sem("cached")
        y_out = sem("y_out")
        ev = {}

        def E(name):
            if name not in ev:
                ev[name] = sem(name)
            return ev[name]

        def reached(place):
            def at(step):
                while place[0] < STEP[step]:
                    yield
            return at

        block = ctx.enter_context(nc.Block())

        def block_done_at(l, b):
            return l * BLOCKS + (b + 1 + RING)

        def slot_free_at(l, b):
            return l * BLOCKS + (b + 1)

        def wait_lo(eng, l, b, dyn=0, pool=None):
            if (b < POOL_BLOCKS) if pool is None else pool:
                eng.wait_ge(lo_pool, l * POOL_BLOCKS + (b + 1) + dyn)
            else:
                eng.wait_ge(lo_dve, l * DVE_BLOCKS + (b - POOL_BLOCKS + 1 + RING) + dyn)

        def drained_at(l, t):
            return l * PER_BANK + (t // 2 + 2)

        def x_part_at(l, k):
            return l * (5 * KC) + (k + 1)

        @block.sync
        def _(sp):
            sp.dma_start(x[:, :, :], dram["x"].rearrange("p (c t) -> p c t", t=T)).then_inc(x_in, 16)
            sp.dma_start(cst[:, :], dram["consts"]).then_inc(const_in, 16)

            def row(name, i):
                return dram[name][bass.ds(sp.snap(i), 1)].rearrange("a p n -> (a p) n")

            def load(src, n_wait, b, l, dyn, units, layer_free=None):
                s = b % RING
                if b < RING:
                    sp.wait_ge(lo_dve, l * DVE_BLOCKS + (b + 1))
                else:
                    wait_lo(sp, l, b - RING, dyn, n_wait)
                if layer_free is not None:
                    sp.wait_ge(E("layer_free"), layer_free)
                sp.dma_start(raw[:, s, 0:units * UNIT], src).then_inc(raw_in[s], 16)

            with sp.Fori(0, DEPTH) as l:
                l1 = sp.snap(l + 1)
                sp.dma_start(prm[:, :], row("params", l)).then_inc(prm_in, 16)
                sp.dma_start(w_lr[:, :, :], row("w_lr", l).rearrange("p (c n) -> p c n", n=16)).then_inc(prm_in, 16)
                for b in range(RING):
                    load(row("w_z", l * NZ + b), True, b, l, 0, 8)
                sp.dma_start(w_a2[0:16, :], row("w_a2", l)).then_inc(prm_in, 16)
                sp.dma_start(w_sp[:, :, :], row("w_sp", l).rearrange("p (g t) -> p g t", g=4)).then_inc(prm_in, 16)
                sp.dma_start(b_sp[:, :, :], row("b_sp", l).rearrange("p (g t) -> p g t", g=4)).then_inc(prm_in, 16)
                sp.dma_start(hist_s[:, :, :, 0:HIST],
                             row("conv_hist", l).rearrange("p (c b t) -> p c b t", c=4, b=DEC_B))\
                    .then_inc(hist_in, 16)
                sp.dma_start(k_hist, row("k_hist", l)).then_inc(kv_in, 16)
                sp.dma_start(kv[:, 1024:2048], row("v_hist", l)).then_inc(kv_in, 16)
                for old, new in (("cache_k", "k_sample"), ("cache_v", "v_sample")):
                    sp.dma_start(dram[new][bass.ds(l, 1)].rearrange("a b t n -> (a b) t n")[:, 0:WIN - DEC_T, :],
                                 dram[old][bass.ds(l, 1)].rearrange("a b t n -> (a b) t n")[:, DEC_T:WIN, :])\
                        .then_inc(cached, 16)
                for b, (t, u, n) in enumerate(z_blocks()):
                    if b >= RING:
                        load(row("w_z", l * NZ + t)[:, u * UNIT:(u + n) * UNIT], True, b, l, 0, n)
                for b in range(RING):
                    load(row("w_gate", l * 32 + b), True, G0 + b, l, 0, 8)
                with sp.Fori(1, 4 * KC // RING) as i:
                    for s in range(RING):
                        n = sp.snap(l * 32 + i * RING + s)
                        load(row("w_gate", n), True, G0 + s, l, i * RING, 8)
                for b in range(2 * KC):
                    load(row("w_branch", l * 16 + b), None, BR0 + b, l, 0, 8)
                for b in range(KC):
                    load(row("w_out", l * 8 + b), None, O0 + b, l, 0, 8)
                sp.wait_ge(E("gv_done"), l1)
                sp.dma_start(row("gmlp_v", l).rearrange("p (c t) -> p c t", c=4), z[:, B_V:B_V + 4, SEQ:T]).then_inc(stored, 16)
                sp.wait_ge(E("state_done"), l1)
                sp.dma_start(row("gla_prompt", l), state[:, :, :].rearrange("p a v -> p (a v)")).then_inc(stored, 16)
                sp.wait_ge(E("state_s_done"), l1)
                sp.dma_start(row("gla_sample", l), kv[:, :]).then_inc(stored, 16)
                sp.wait_ge(E("conv_h"), l1)
                sp.dma_start(row("conv_prompt", l).rearrange("p (c t) -> p c t", c=4), hist_p[:, :, SEQ:SEQ + HIST]).then_inc(stored, 16)
                sp.dma_start(row("conv_sample", l), hist_s[:, :, :, :].rearrange("p c b t -> p (c b t)")).then_inc(stored, 16)
                sp.wait_ge(E("qk_done"), l1)
                sp.dma_start(row("k_prompt", l), z[:, D_K, WIN:SEQ]).then_inc(stored, 16)
                sp.dma_start(row("v_prompt", l), z[:, D_V, WIN:SEQ]).then_inc(stored, 16)
                sp.wait_ge(E("tok_copied"), l1)
                for i, new in enumerate(("v_sample", "k_sample")):
                    sp.dma_start(dram[new][bass.ds(l, 1)].rearrange("a b t n -> (a b) t n")[:, WIN - DEC_T:WIN, :],
                                 vs[0:TS, i, :]).then_inc(stored, 16)
                with sp.Fori(0, 2 * HC // RING) as i:
                    for s in range(RING):
                        n = sp.snap(l * 44 + i * RING + s)
                        load(row("w_up", n), False, U0 + s, l, i * RING, 8)
                for d in range(KC):
                    at = 0
                    for q, n in enumerate(DOWN_UNITS):
                        free = d == KC - 1 and q == 2
                        load(row("w_down", l * KC + d)[:, at * UNIT:(at + n) * UNIT], None, DN0 + 3 * d + q, l, 0, n,
                             l1 if free else None)
                        at += n
            sp.wait_ge(bank_free[0], (DEPTH - 1) * PER_BANK + (TILES - 2) // 2 + 2)
            sp.wait_ge(bank_free[1], (DEPTH - 1) * PER_BANK + (TILES - 1) // 2 + 2)
            sp.dma_start(dram["y"].rearrange("p (c t) -> p c t", t=T), x[:, :, :]).then_inc(y_out, 16)
            sp.wait_ge(y_out, 16)

        @block.tensor
        def _(pe):
            place = [0]
            at = reached(place)

            def split_mm(out, slot, u, rh, rl, start, stop):
                wh = w_hi[:, slot, u * UNIT:(u + 1) * UNIT]
                wl = w_lo[:, slot, u * UNIT:(u + 1) * UNIT]
                pe.matmul(out, wh, rh, start=start, stop=False)
                pe.matmul(out, wh, rl, start=False, stop=False)
                return pe.matmul(out, wl, rh, start=False, stop=stop)

            def bank_wait(l, t, dyn=0):
                pe.wait_ge(bank_free[t % 2], l * PER_BANK + (t // 2 + 1) + dyn)

            def sum_chunks(bank, src, n, event, wait_each=None):
                for k in range(n):
                    if wait_each:
                        wait_each(k)
                    mm = pe.matmul(ps[:, bank, 0:T], c("ones"), src[:, k, :], start=k == 0, stop=k == n - 1)
                mm.then_inc(E(event), 1)

            def mixers(l, l1):
                yield from at("qk_sums")
                pe.wait_ge(E("qk_sq"), l1)
                pe.wait_ge(E("lr_ready"), l1)
                for k in range(5):
                    mm = pe.matmul(ps[:, 2 + k, 0:T], c("heads"), sq5[:, k, :], start=True, stop=True)
                mm.then_inc(E("qk_sums"), 1)
                yield from at("qk_turned")
                pe.wait_ge(E("qk_normed"), l1)
                for k in range(5):
                    mm = pe.matmul(ps[:, 2 + k, 0:T], c("turn"), z[:, D_Q + k, :], start=True, stop=True)
                mm.then_inc(E("qk_turned"), 1)
                yield from at("scores0")
                pe.wait_ge(E("qk_done"), l1)
                for k in range(2):
                    pe.transpose(ps[:, 7, k * P:(k + 1) * P], z[:, D_V, k * P:(k + 1) * P], c("ident"))
                pe.transpose(ps[0:TS, 7, 2 * P:3 * P], z[:, D_V, SEQ:T], c("ident"))
                pe.transpose(ps[0:TS, 7, 3 * P:4 * P], z[:, D_K, SEQ:T], c("ident")).then_inc(E("tok_turned"), 1)
                for kvh in range(2):
                    r = slice(64 * kvh, 64 * kvh + 64)
                    for j in range(4):
                        mm = pe.matmul(ps[:, 2 + kvh, j * P:(j + 1) * P], z[r, D_Q + j, 0:P], z[r, D_K, 0:P],
                                       start=True, stop=True)
                mm.then_inc(E("scores0"), 1)
                yield from at("scores1")
                pe.wait_ge(E("tok_copied"), l1)
                for kvh in range(2):
                    r = slice(64 * kvh, 64 * kvh + 64)
                    for j in range(4):
                        mm = pe.matmul(ps[:, 4 + 2 * kvh + j // 2, (j % 2) * 256:(j % 2) * 256 + 256],
                                       z[r, D_Q + j, P:SEQ], z[r, D_K, 0:SEQ], start=True, stop=True)
                mm.then_inc(E("scores1"), 1)
                yield from at("probs_turned")
                pe.wait_ge(E("probs0"), l1)
                for h in range(8):
                    mm = pe.transpose(ps[:, 2 + h // 4, (h % 4) * P:(h % 4 + 1) * P], prob0[:, h, :], c("ident"))
                mm.then_inc(E("probs0_turned"), 1)
                pe.wait_ge(E("probs1"), l1)
                for a in range(2):
                    for h in range(8):
                        mm = pe.transpose(ps[:, 4 + 2 * a + h // 4, (h % 4) * P:(h % 4 + 1) * P],
                                          prob1[:, h, a * P:(a + 1) * P], c("ident"))
                mm.then_inc(E("probs1_turned"), 1)
                yield from at("prompt_pv")
                pe.wait_ge(E("probs1_copied"), l1)
                for kvh in range(2):
                    r = slice(64 * kvh, 64 * kvh + 64)
                    pe.matmul(ps[r, 2, :], vt[:, 0, r], prob0_t[:, 512 * kvh:512 * kvh + 512], start=True, stop=True)
                    for a in range(2):
                        mm = pe.matmul(ps[r, 3, :], vt[:, a, r], prob1_t[:, a, 512 * kvh:512 * kvh + 512],
                                       start=a == 0, stop=a == 1)
                mm.then_inc(E("prompt_pv"), 1)
                pe.wait_ge(kv_in, l1 * 32)
                pe.wait_ge(E("q_smp"), l1)
                for kvh in range(2):
                    r = slice(64 * kvh, 64 * kvh + 64)
                    for half in range(2):
                        mm = pe.matmul(ps[:, 4 + 2 * kvh + half, :], q_smp[r, :], k_hist[r, half * 512:half * 512 + 512],
                                       start=True, stop=True)
                mm.then_inc(E("smp_hist"), 1)
                yield from at("smp_new")
                pe.wait_ge(E("prompt_od"), l1)
                for kvh in range(2):
                    r = slice(64 * kvh, 64 * kvh + 64)
                    mm = pe.matmul(ps[:, 2 + kvh, 0:TS], q_smp[r, :], z[r, D_K, SEQ:T], start=True, stop=True)
                mm.then_inc(E("smp_new"), 1)
                yield from at("probs_s_turned")
                pe.wait_ge(E("probs_s"), l1)
                for kvh in range(2):
                    for b in range(DEC_B):
                        pe.transpose(ps[:, 4 + 2 * kvh + b // 4, (b % 4) * P:(b % 4 + 1) * P],
                                     prob_s[:, kvh, b * P:(b + 1) * P], c("ident"))
                for kvh in range(2):
                    mm = pe.transpose(ps[0:TS, 2, kvh * P:(kvh + 1) * P], prob_s[:, kvh, 1024:1056], c("ident"))
                mm.then_inc(E("probs_s_turned"), 1)
                yield from at("smp_pv")
                pe.wait_ge(E("probs_s_copied"), l1)
                for kvh in range(2):
                    r = slice(64 * kvh, 64 * kvh + 64)
                    pe.matmul(ps[r, 3, 0:P], vs[0:TS, 0, r], prob_nt[0:TS, kvh, :], start=True, stop=False,
                              skip_group_check=True)
                    for b in range(DEC_B):
                        cols = slice(DEC_T * b, DEC_T * b + DEC_T)
                        mm = pe.matmul(ps[r, 3, 0:P].rearrange("p (j n) -> p j n", j=4)[:, :, cols], v_hist[:, b, r],
                                       prob_st[:, kvh, b, :].rearrange("p (j n) -> p j n", j=4)[:, :, cols],
                                       start=False, stop=b == DEC_B - 1, skip_group_check=True)
                mm.then_inc(E("smp_pv"), 1)
                yield from at("decay_in")
                pe.wait_ge(E("lr_ready"), l1)
                pe.wait_ge(prm_in, l1 * 80)
                for k in range(2):
                    mm = pe.matmul(ps[:, 4 + k, 0:T], w_a2[0:16, k * P:(k + 1) * P], lr[0:16, :], start=True, stop=True)
                mm.then_inc(E("decay_in"), 1)
                pe.wait_ge(E("smp_od"), l1)
                for h in range(4):
                    for a in range(2):
                        pe.transpose(ps[:, 6 + a, h * P:(h + 1) * P], z[:, A_V + h, a * P:(a + 1) * P], c("ident"))
                for h in range(4):
                    mm = pe.transpose(ps[0:TS, 2, h * P:(h + 1) * P], z[:, A_V + h, SEQ:T], c("ident"))
                mm.then_inc(E("v_turned"), 1)
                yield from at("att_in")
                pe.wait_ge(E("v_copied"), l1)
                pe.wait_ge(E("k_last_done"), l1)
                for a in range(2):
                    for k in range(2):
                        pe.transpose(ps[:, 6, (2 * a + k) * P:(2 * a + k + 1) * P], z[:, A_K + k, a * P:(a + 1) * P],
                                     c("ident"))
                for k in range(2):
                    mm = pe.transpose(ps[0:TS, 7, k * P:(k + 1) * P], z[:, A_K + k, SEQ:T], c("ident"))
                mm.then_inc(E("k_turned"), 1)
                for par in range(2):
                    r = slice(64 * par, 64 * par + 64)
                    for hp in range(2):
                        for ch in range(NSEG):
                            o = slice(64 * (ch % 2), 64 * (ch % 2) + 64)
                            col = (hp * 2 + ch // 2) * 64
                            tok = slice(ch * 64, ch * 64 + 64)
                            pe.matmul(ps[o, 4 + par, col:col + 64], k_neg[r, hp, tok], qz[r, 2 * hp + par, tok],
                                      start=True, stop=True)
                        mm = pe.matmul(ps[0:TS, 4 + par, 256 + hp * TS:256 + hp * TS + TS], k_neg[r, hp, SEQ:T],
                                       qz[r, 2 * hp + par, SEQ:T], start=True, stop=True)
                mm.then_inc(E("att_in"), 1)
                yield from at("chunks")
                pe.wait_ge(E("att_done"), l1)
                pe.wait_ge(E("k_copied"), l1)
                for ch in range(NSEG):
                    a, rows = ch // 2, slice(64 * (ch % 2), 64 * (ch % 2) + 64)
                    for k in range(2):
                        mm = pe.matmul(ps[:, 4 + ch % 2, k * 256:k * 256 + 256], k_tok[rows, a, k * P:(k + 1) * P],
                                       v_tok[rows, a, k * 256:k * 256 + 256], start=True, stop=True)
                    mm.then_inc(E("update"), 1)
                    if ch >= 1:
                        pe.wait_ge(E("state_step"), l * NSEG + ch)
                    for h in range(4):
                        out = ps[:, 2 + a, h * P + 64 * (ch % 2):h * P + 64 * (ch % 2) + 64]
                        mm = pe.matmul(out, v_tok[:, a, h * P:(h + 1) * P], attz[:, h, a, 64 * (ch % 2):64 * (ch % 2) + 64],
                                       start=True, stop=ch == 0)
                        if ch >= 1:
                            mm = pe.matmul(out, state[:, h // 2, :], qz[:, h, ch * 64:ch * 64 + 64], start=False, stop=True)
                    mm.then_inc(E("chunk_out"), 1)
                yield from at("smp_out")
                pe.wait_ge(state_in, l1 * 16)
                for h in range(4):
                    pe.matmul(ps[:, 6, h * TS:h * TS + TS], v_tok_s[0:TS, h * P:(h + 1) * P], att_s[0:TS, h, :],
                              start=True, stop=False, skip_group_check=True)
                    for b in range(DEC_B):
                        cols = slice(h * TS + DEC_T * b, h * TS + DEC_T * b + DEC_T)
                        mm = pe.matmul(ps[:, 6, cols], s_smp[:, b, h // 2, :],
                                       qz[:, h, SEQ + DEC_T * b:SEQ + DEC_T * b + DEC_T], start=False,
                                       stop=b == DEC_B - 1, skip_group_check=True)
                mm.then_inc(E("smp_out"), 1)
                yield from at("smp_update")
                pe.wait_ge(E("k_own_done"), l1)
                pe.wait_ge(E("state_done"), l1)
                for b in range(DEC_B):
                    if b >= 2:
                        pe.wait_ge(E("smp_added"), l * DEC_B + b - 1)
                    for k in range(2):
                        mm = pe.matmul(ps[:, 4 + b % 2, k * 256:k * 256 + 256], k_own[0:TS, b, k * P:(k + 1) * P],
                                       v_tok_s[0:TS, k * 256:k * 256 + 256], start=True, stop=True)
                    mm.then_inc(E("smp_update"), 1)
                yield from at("gla_sums")
                pe.wait_ge(E("gla_sq"), l1)
                for h in range(4):
                    mm = pe.matmul(ps[:, (2, 3, 6, 7)[h], 0:T], c("ones"), z[:, A_V + h, :], start=True, stop=True)
                mm.then_inc(E("gla_sums"), 1)
                yield from at("gm_mean")
                for k in range(4):
                    if k == 0:
                        pe.wait_ge(E("v_gelu"), l1)
                        pe.wait_ge(E("smp_added"), l * DEC_B + DEC_B)
                    mm = pe.matmul(ps[:, 4, 0:T], c("ones"), z[:, B_V + k, :], start=k == 0, stop=k == 3)
                mm.then_inc(E("gm_mean"), 1)
                yield from at("gm_var")
                pe.wait_ge(E("gm_sq"), l1)
                sum_chunks(5, g_sq, 4, "gm_var")
                yield from at("gv_turned")
                pe.wait_ge(E("gv_done"), l1)
                for g in range(4):
                    for a in range(2):
                        pe.transpose(ps[:, 2 + a, g * P:(g + 1) * P], z[:, B_V + g, a * P:(a + 1) * P], c("ident"))
                    mm = pe.transpose(ps[0:TS, 6, g * P:(g + 1) * P], z[:, B_V + g, SEQ:T], c("ident"))
                mm.then_inc(E("gv_turned"), 1)
                pe.wait_ge(E("w_sp_masked"), l1)
                for g in range(4):
                    mm = pe.matmul(ps[0:TS, 7, g * DEC_T:g * DEC_T + DEC_T], c("rep", TS)[0:P], w_sp[:, g, 0:DEC_T],
                                   start=True, stop=True)
                mm.then_inc(E("corner"), 1)
                yield from at("mixed")
                pe.wait_ge(E("gv_copied"), l1)
                pe.wait_ge(E("w_bd_done"), l1)
                for g in range(4):
                    for a in range(2):
                        pe.matmul(ps[:, 4 + a, g * P:(g + 1) * P], gv_tok[:, a, g * P:(g + 1) * P], w_sp[:, g, :],
                                  start=True, stop=True)
                    mm = pe.matmul(ps[:, 7, g * TS:g * TS + TS], gv_tok_s[0:TS, g * P:(g + 1) * P], w_bd[0:TS, g, :],
                                   start=True, stop=True)
                mm.then_inc(E("mixed"), 1)
                yield from at("cv_mean")
                pe.wait_ge(E("conv_done"), l1)
                pe.wait_ge(E("gv_copied"), l1)
                sum_chunks(2, z[:, C_A:C_A + 4, :], 4, "cv_mean")
                yield from at("cv_var")
                pe.wait_ge(E("cv_sq"), l1)
                sum_chunks(3, g_sq, 4, "cv_var")

            pe.wait_ge(const_in, 16)
            with pe.Fori(0, DEPTH) as l:
                l1 = pe.snap(l + 1)
                sum_chunks(7, xn, KC, "n1_sums", lambda k: pe.wait_ge(E("n1_sq"), l * KC + k + 1))
                mix = mixers(l, l1)
                pe.wait_ge(prm_in, l1 * 80)
                for k in range(KC):
                    if k == 0:
                        pe.wait_ge(xn_done, l * (2 * KC) + KC)
                    mm = pe.matmul(ps[0:16, 6, 0:T], w_lr[:, k, :], xn[:, k, :], start=k == 0, stop=k == KC - 1)
                mm.then_inc(E("lr_sums"), 1)
                for b, (t, u0, n) in enumerate(z_blocks()):
                    wait_lo(pe, l, Z0 + b)
                    if u0 == 0:
                        bank_wait(l, TZ + t)
                    for u in range(n):
                        if b == 0:
                            pe.wait_ge(xl_done, x_part_at(l, u))
                        mm = split_mm(ps[:, t % 2, 0:T], b % RING, u, x_hi[:, u0 + u, :], x_lo[:, u0 + u, :],
                                      u0 + u == 0, u0 + u == KC - 1)
                    mm.then_inc(blocks_done, 1)
                    place[0] = b
                    next(mix, None)
                for t in range(4 * KC):
                    wait_lo(pe, l, G0 + t)
                    bank_wait(l, TG + t)
                    for u in range(KC):
                        mm = split_mm(ps[:, t % 2, 0:T], t % RING, u, x_hi[:, u, :], x_lo[:, u, :], u == 0, u == KC - 1)
                    mm.then_inc(blocks_done, 1)
                    place[0] = G0 + t
                    next(mix, None)
                for _ in mix:
                    pass
                for b in range(2 * KC):
                    i = b // 4
                    wait_lo(pe, l, BR0 + b)
                    for d in range(2):
                        t = 2 * b + d
                        bank_wait(l, TB + t)
                        for u in range(4):
                            if t % 8 == 0:
                                pe.wait_ge(xl_done, x_part_at(l, KC + 4 * i + u))
                            k = 4 * (i % 2) + u
                            mm = split_mm(ps[:, t % 2, 0:T], b % RING, 4 * d + u, x_hi[:, k, :], x_lo[:, k, :],
                                          u == 0, u == 3)
                    mm.then_inc(blocks_done, 1)
                for t in range(KC):
                    wait_lo(pe, l, O0 + t)
                    bank_wait(l, TO + t)
                    for u in range(KC):
                        if t == 0:
                            pe.wait_ge(xl_done, x_part_at(l, 3 * KC + u))
                        mm = split_mm(ps[:, t % 2, 0:T], t % RING, u, x_hi[:, u, :], x_lo[:, u, :], u == 0, u == KC - 1)
                    mm.then_inc(blocks_done, 1)
                sum_chunks(7, xn, KC, "n2_sums", lambda k: pe.wait_ge(E("n2_sq"), l * KC + k + 1))
                with pe.Fori(0, 2 * HC // RING) as i:
                    n = pe.snap(i * RING)
                    pe.wait_ge(xl_done, x_part_at(l, 5 * KC - 1))
                    for s in range(RING):
                        wait_lo(pe, l, U0 + s, n)
                        bank_wait(l, TU + s, i * (RING // 2))
                        for u in range(KC):
                            mm = split_mm(ps[:, s % 2, 0:T], s, u, x_hi[:, u, :], x_lo[:, u, :], u == 0, u == KC - 1)
                        mm.then_inc(blocks_done, 1)
                for t in range(KC):
                    done = 0
                    for q, n in enumerate(DOWN_UNITS):
                        b = DN0 + 3 * t + q
                        wait_lo(pe, l, b)
                        if q == 0:
                            bank_wait(l, TD + t)
                        for u in range(n):
                            if t == 0:
                                pe.wait_ge(hid_lo, l * HC + (done + u + 1))
                            mm = split_mm(ps[:, t % 2, 0:T], b % RING, u, h_hi[:, done + u, :], h_lo[:, done + u, :],
                                          done + u == 0, done + u == HC - 1)
                        done += n
                        mm.then_inc(blocks_done, 1)

        @block.scalar
        def _(act):
            place = [0]
            at = reached(place)

            chain = [0]

            def link(ins, l):
                ins.then_inc(act_link, 1)
                chain[0] += 1
                act.wait_ge(act_link, l * ACT_LINKS + chain[0])

            def split(l, b, dyn=0, dyn_slot=0):
                s = b % RING
                act.wait_ge(raw_in[s], l * (16 * (BLOCKS // RING)) + 16 * (b // RING + 1) + dyn_slot)
                act.wait_ge(blocks_done, slot_free_at(l, b) + dyn)
                act.activation(w_hi[:, s, :], raw[:, s, :], ACT.Copy).then_inc(hi_done, 1)

            def drain(l, b, t, out, bias):
                act.wait_ge(blocks_done, block_done_at(l, b))
                act.activation(out, ps[:, t % 2, 0:T], ACT.Identity, bias=bias).then_inc(bank_free[t % 2], 1)

            def mixers(l, l1):
                yield from at("c_gate")
                act.wait_ge(bank_free[0], drained_at(l, TZ + C_G + 2))
                act.wait_ge(bank_free[1], drained_at(l, TZ + C_G + 3))
                act.activation(z[:, C_G:C_G + 4, :], z[:, C_G:C_G + 4, :], ACT.Sigmoid).then_inc(E("c_gate"), 1)
                yield from at("qk_sq")
                act.wait_ge(bank_free[0], drained_at(l, TZ + D_K))
                act.wait_ge(E("conv_samples"), l1)
                act.activation(sq5, z[:, D_Q:D_Q + 5, :], ACT.Square).then_inc(E("qk_sq"), 1)
                yield from at("qk_rstd")
                act.wait_ge(E("qk_inv"), l1)
                act.activation(r5, r5, ACT.Sqrt).then_inc(E("qk_rstd"), 1)
                yield from at("tok_copied")
                act.wait_ge(E("tok_turned"), l1)
                act.activation(vt[:, :, :].rearrange("p a n -> p (a n)"), ps[:, 7, 0:2 * P], ACT.Copy)
                act.activation(vs[0:TS, :, :].rearrange("p a n -> p (a n)"), ps[0:TS, 7, 2 * P:4 * P], ACT.Copy)\
                    .then_inc(E("tok_copied"), 1)
                act.activation(q_smp[:, :].rearrange("p (j t) -> p j t", j=4), z[:, D_Q:D_Q + 4, SEQ:T], ACT.Copy)\
                    .then_inc(E("q_smp"), 1)
                yield from at("exp0")
                for blk, src, sums in ((0, prob0, "exp0"), (1, prob1, "exp1")):
                    act.wait_ge(E(f"shift{blk}"), l1)
                    for h in range(8):
                        ins = act.activation(src[:, h, :], src[:, h, :], ACT.Exp, bias=small[:, 1, 8 * blk + h:8 * blk + h + 1],
                                             accum_out=small[:, 3, 8 * blk + h:8 * blk + h + 1])
                    ins = act.activation(small[:, 2, 8 * blk:8 * blk + 8], small[:, 2, 8 * blk:8 * blk + 8], ACT.Exp)
                    ins.then_inc(E(sums), 1)
                yield from at("probs_copied")
                act.wait_ge(E("probs0_turned"), l1)
                act.activation(prob0_t, ps[:, 2:4, :], ACT.Copy)
                act.wait_ge(E("probs1_turned"), l1)
                act.activation(prob_t[:, 1024:3072], ps[:, 4:8, :], ACT.Copy).then_inc(E("probs1_copied"), 1)
                yield from at("prompt_od")
                act.wait_ge(E("prompt_pv"), l1)
                act.activation(z[:, D_Q:D_Q + 4, 0:P], ps[:, 2, :].rearrange("p (j q) -> p j q", j=4), ACT.Copy)
                act.activation(z[:, D_Q:D_Q + 4, P:SEQ], ps[:, 3, :].rearrange("p (j q) -> p j q", j=4), ACT.Copy)\
                    .then_inc(E("prompt_od"), 1)
                yield from at("exp_s")
                act.wait_ge(E("shift_s"), l1)
                for kvh in range(2):
                    act.activation(prob_s[:, kvh, :], prob_s[:, kvh, :], ACT.Exp, bias=small[:, 1, 16 + kvh:17 + kvh],
                                   accum_out=small[:, 3, 16 + kvh:17 + kvh])
                act.activation(small[:, 2, 16:18], small[:, 2, 16:18], ACT.Exp).then_inc(E("exp_s"), 1)
                yield from at("gelu")
                act.wait_ge(bank_free[1], drained_at(l, TZ + B_V + 3))
                act.wait_ge(bank_free[0], drained_at(l, TZ + B_V + 2))
                act.activation(z[:, B_V:B_V + 4, :], z[:, B_V:B_V + 4, :], ACT.Gelu).then_inc(E("v_gelu"), 1)
                act.activation(z[:, B_U:B_U + 4, :], z[:, B_U:B_U + 4, :], ACT.Gelu).then_inc(E("u_gelu"), 1)
                yield from at("probs_s_copied")
                act.wait_ge(E("probs_s_turned"), l1)
                act.activation(prob_t[:, 0:2048], ps[:, 4:8, :], ACT.Copy)
                act.activation(prob_t[0:TS, 2048:2048 + 2 * P], ps[0:TS, 2, 0:2 * P], ACT.Copy)\
                    .then_inc(E("probs_s_copied"), 1)
                yield from at("smp_od")
                act.wait_ge(E("smp_pv"), l1)
                act.activation(z[:, D_Q:D_Q + 4, SEQ:T], ps[:, 3, 0:P].rearrange("p (j q) -> p j q", j=4), ACT.Copy)\
                    .then_inc(E("smp_od"), 1)
                act.dma_start(kv[:, :], dram["state"][bass.ds(l, 1)].rearrange("a p n -> (a p) n")).then_inc(state_in, 16)
                yield from at("decay_log")
                act.wait_ge(E("decay_in"), l1)
                for k in range(2):
                    ins = act.activation(e_last[:, k, :], ps[:, 4 + k, 0:T], ACT.Identity, bias=p("b_alpha", k))
                ins.then_inc(E("decay_y"), 1)
                act.wait_ge(E("decay_y"), l1)
                link(act.activation(e_pos, e_last, ACT.Abs), l)
                link(act.activation(e_pos, e_pos, ACT.Exp, scale=-1.0), l)
                act.activation(e_pos, e_pos, ACT.Ln, bias=1.0).then_inc(E("decay_log"), 1)
                act.wait_ge(E("v_turned"), l1)
                act.activation(v_tok, ps[:, 6:8, :], ACT.Copy)
                act.activation(v_tok_s[0:TS, :], ps[0:TS, 2, :], ACT.Copy).then_inc(E("v_copied"), 1)
                yield from at("decay_exp")
                act.wait_ge(E("decay_sum"), l1)
                act.activation(e_pos, bcum, ACT.Exp, scale=1.0 / 16).then_inc(E("e_pos_done"), 1)
                act.activation(k_neg, bcum, ACT.Exp, scale=-1.0 / 16).then_inc(E("e_neg_done"), 1)
                act.wait_ge(E("last_diff"), l1)
                act.activation(e_last, e_last, ACT.Exp, scale=1.0 / 16).then_inc(E("e_last_done"), 1)
                yield from at("k_copied")
                act.wait_ge(E("k_turned"), l1)
                act.activation(k_tok, ps[:, 6, :].rearrange("p (a n) -> p a n", a=2), ACT.Copy)
                act.activation(k_tok_s[0:TS, :], ps[0:TS, 7, 0:2 * P], ACT.Copy).then_inc(E("k_copied"), 1)
                yield from at("gla_o")
                for a in range(2):
                    act.wait_ge(E("chunk_out"), l * NSEG + 2 * a + 2)
                    act.activation(gla_o[:, :, a * P:(a + 1) * P], ps[:, 2 + a, :].rearrange("p (h i) -> p h i", h=4), ACT.Copy)
                act.wait_ge(E("smp_out"), l1)
                link(act.activation(gla_o[:, :, SEQ:T], ps[:, 6, 0:4 * TS].rearrange("p (h i) -> p h i", h=4), ACT.Copy), l)
                act.activation(z[:, A_V:A_V + 4, :], gla_o, ACT.Square).then_inc(E("gla_sq"), 1)
                act.activation(z[:, A_R:A_R + 4, :], z[:, A_R:A_R + 4, :], ACT.Silu).then_inc(E("r_silu"), 1)
                yield from at("gla_rstd")
                act.wait_ge(E("gla_inv"), l1)
                act.activation(g_tmp, g_tmp, ACT.Sqrt).then_inc(E("gla_rstd"), 1)
                yield from at("gm_sq")
                act.wait_ge(E("gm_centred"), l1)
                act.wait_ge(E("a_out"), l1)
                act.activation(g_sq, z[:, B_V:B_V + 4, :], ACT.Square).then_inc(E("gm_sq"), 1)
                yield from at("gv_done")
                act.wait_ge(E("gm_inv"), l1)
                act.activation(rs[:, :], rs[:, :], ACT.Sqrt).then_inc(E("gm_rstd"), 1)
                act.wait_ge(E("gm_scaled"), l1)
                for k in range(4):
                    ins = act.activation(z[:, B_V + k, :], z[:, B_V + k, :], ACT.Identity, scale=p("gmlp_g", k),
                                         bias=p("gmlp_b", k))
                ins.then_inc(E("gv_done"), 1)
                yield from at("gv_copied")
                act.wait_ge(E("gv_turned"), l1)
                act.activation(gv_tok, ps[:, 2:4, :], ACT.Copy)
                act.activation(gv_tok_s[0:TS, :], ps[0:TS, 6, :], ACT.Copy).then_inc(E("gv_copied"), 1)
                yield from at("cv_sq")
                act.wait_ge(E("cv_centred"), l1)
                act.wait_ge(E("b_out"), l1)
                act.activation(g_sq, z[:, C_A:C_A + 4, :], ACT.Square).then_inc(E("cv_sq"), 1)
                yield from at("c_out")
                act.wait_ge(E("cv_inv"), l1)
                act.activation(rs[:, :], rs[:, :], ACT.Sqrt).then_inc(E("cv_rstd"), 1)
                act.wait_ge(E("cv_scaled"), l1)
                for k in range(4):
                    ins = act.activation(z[:, C_A + k, :], z[:, C_A + k, :], ACT.Silu, scale=p("conv_g", k),
                                         bias=p("conv_lb", k))
                ins.then_inc(E("c_out"), 1)

            def input_part(l, k, src):
                act.activation(x_hi[:, k_slot(k), :], src, ACT.Copy).then_inc(xh_done, 1)

            def norm(l, l1, which, count):
                for k in range(KC):
                    act.activation(xn[:, k, :], x[:, k, :], ACT.Square).then_inc(E(f"n{which}_sq"), 1)
                act.wait_ge(E(f"n{which}_inv"), l1)
                act.activation(rs[:, :], rs[:, :], ACT.Sqrt).then_inc(E(f"n{which}_rstd"), 1)
                for k in range(KC):
                    act.wait_ge(xn_done, l * (2 * KC) + (which - 1) * KC + k + 1)
                    input_part(l, count + k, xn[:, k, :])

            act.wait_ge(x_in, 16)
            with act.Fori(0, DEPTH) as l:
                chain[0] = 0
                l1 = act.snap(l + 1)
                for b in range(3):
                    split(l, b)
                act.wait_ge(bank_free[0], l * PER_BANK + 1)
                act.wait_ge(bank_free[1], l * PER_BANK + 1)
                norm(l, l1, 1, 0)
                mix = mixers(l, l1)
                act.wait_ge(prm_in, l1 * 80)
                done = None
                for b, (t, u0, n) in enumerate(z_blocks()):
                    split(l, b + 3)
                    if done is not None:
                        drain(l, Z0 + b - 1, TZ + done, z[:, done, :], p("b_in", done))
                    done = t if u0 + n == KC else None
                    place[0] = b
                    next(mix, None)
                for t in range(4 * KC):
                    split(l, G0 + t + 3)
                    if t == 0:
                        drain(l, G0 - 1, TZ + NZ - 1, z[:, NZ - 1, :], p("b_in", NZ - 1))
                    else:
                        drain(l, G0 + t - 1, TG + t - 1, gate[:, t - 1, :], p("b_gate", t - 1))
                    place[0] = G0 + t
                    next(mix, None)
                drain(l, BR0 - 1, TB - 1, gate[:, 4 * KC - 1, :], p("b_gate", 4 * KC - 1))
                for _ in mix:
                    pass
                act.wait_ge(blocks_done, block_done_at(l, BR0 - 1))
                act.wait_ge(bank_free[0], drained_at(l, TB - 2))
                act.wait_ge(bank_free[1], drained_at(l, TB - 1))
                branch_in = ((A_R, "a_out"), (B_U, "b_out"), (C_A, "c_out"), (D_Q, "smp_od"))
                for i in range(4):
                    tile, event = branch_in[i]
                    act.wait_ge(E(event), l1)
                    for k in range(4):
                        if i >= 2 and k == 0:
                            act.wait_ge(blocks_done, block_done_at(l, BR0 + 4 * (i - 2) + 3))
                        input_part(l, KC + 4 * i + k, z[:, tile + k, :])
                    if i == 0:
                        for g in range(4):
                            act.activation(gate[:, g * KC:(g + 1) * KC, :], gate[:, g * KC:(g + 1) * KC, :], ACT.Sigmoid)\
                                .then_inc(E("gates_done"), 1)
                    if i >= 1:
                        for b in range(4):
                            split(l, BR0 + 4 * (i - 1) + b + 3)
                for b in range(4):
                    split(l, BR0 + 4 * 3 + b + 3)
                for k in range(KC):
                    if k == 4:
                        act.wait_ge(blocks_done, block_done_at(l, BR0 + 15))
                    act.wait_ge(summed, l * (3 * KC) + (2 * KC + k + 1))
                    input_part(l, 3 * KC + k, gate[:, k, :])
                for t in range(KC):
                    split(l, O0 + t + 3)
                for k in range(2):
                    act.wait_ge(bank_free[k], drained_at(l, TO + KC - 2 + k))
                act.wait_ge(stored, l1 * (16 * STORES_PER_LAYER))
                norm(l, l1, 2, 4 * KC)
                with act.Fori(0, 2 * HC // RING) as i:
                    n = act.snap(i * RING)
                    for s in range(RING):
                        bb = U0 + s + 3
                        split(l, bb, n, i * 16)
                        if s % 2 == 0:
                            act.wait_ge(hid_free, l * HC + (s // 2 + 1) + i * 2)
                            act.wait_ge(blocks_done, block_done_at(l, U0 + s) + n)
                            act.activation(gate_s[:, s // 2, :], ps[:, 0, 0:T], ACT.Silu).then_inc(bank_free[0], 1)
                        else:
                            act.wait_ge(bank_free[1], l * PER_BANK + ((TU + s) // 2 + 2) + i * 2)
                            act.activation(h_hi[:, bass.ds(i * 2 + s // 2, 1), :], hidden[:, s // 2:s // 2 + 1, :], ACT.Copy)\
                                .then_inc(hid_hi, 1)
                for b in range(DN0 + 3, BLOCKS):
                    split(l, b)
                assert chain[0] == ACT_LINKS, chain[0]

        def branch_blocks(dve, split, l, i):
            for b in range(4):
                split(l, BR0 + 4 * i + b + 3)
                dve.wait_ge(blocks_done, block_done_at(l, BR0 + 4 * i + b))
                if b == 0:
                    dve.wait_ge(E("gates_done"), l * 4 + i + 1)
                for d in range(2):
                    t = 8 * i + 2 * b + d
                    dve.tensor_tensor(gate[:, t, :], ps[:, t % 2, 0:T], gate[:, t, :], ALU.mult).then_inc(bank_free[t % 2], 1)

        @block.vector
        def _(dve):
            chain = [0]

            def link(ins, l):
                ins.then_inc(dve_link, 1)
                chain[0] += 1
                dve.wait_ge(dve_link, l * DVE_LINKS + chain[0])

            def split(l, b, dyn=0):
                if b >= POOL_BLOCKS:
                    s = b % RING
                    dve.wait_ge(hi_done, l * BLOCKS + (b + 1) + dyn)
                    dve.tensor_tensor(w_lo[:, s, :], raw[:, s, :], w_hi[:, s, :].bitcast(f32), ALU.subtract)\
                        .then_inc(lo_dve, 1)

            def input_part(l, k, src):
                dve.wait_ge(xh_done, x_part_at(l, k))
                dve.tensor_tensor(x_lo[:, k_slot(k), :], src, x_hi[:, k_slot(k), :].bitcast(f32), ALU.subtract)\
                    .then_inc(xl_done, 1)

            def inverse(l, l1, sums, n, out, event, eps):
                link(dve.tensor_scalar(out, sums, 1.0 / n, eps, ALU.mult, ALU.add), l)
                dve.reciprocal(out, out).then_inc(E(event), 1)

            def norm(l, l1, which, count):
                dve.wait_ge(E(f"n{which}_sums"), l1)
                inverse(l, l1, ps[:, 7, 0:T], D_MODEL, rs[:, :], f"n{which}_inv", 1e-6)
                dve.wait_ge(E(f"n{which}_rstd"), l1)
                for k in range(KC):
                    dve.scalar_tensor_tensor(out=xn[:, k, :], in0=x[:, k, :], scalar=p(f"norm{which}", k), in1=rs[:, :],
                                             op0=ALU.mult, op1=ALU.mult).then_inc(xn_done, 1)
                for k in range(KC):
                    input_part(l, count + k, xn[:, k, :])

            def bcast(ap, n):
                return ap.unsqueeze(1).to_broadcast([P, n, ap.shape[1]])

            def conv(l, l1):
                dve.wait_ge(E("c_gate"), l1)
                dve.wait_ge(hist_in, l1 * 16)
                dve.tensor_tensor(hist_p[:, :, HIST:HIST + SEQ], z[:, C_A:C_A + 4, 0:SEQ], z[:, C_G:C_G + 4, 0:SEQ], ALU.mult)
                dve.tensor_tensor(hist_s[:, :, :, HIST:EXT], z[:, C_A:C_A + 4, SEQ:T].rearrange("p c (b t) -> p c b t", t=DEC_T),
                                  z[:, C_G:C_G + 4, SEQ:T].rearrange("p c (b t) -> p c b t", t=DEC_T), ALU.mult)\
                    .then_inc(E("conv_h"), 1)
                yield
                dve.wait_ge(E("conv_h"), l1)
                for k in range(4):
                    taps = p("conv_w", k * CONV_K, CONV_K)
                    link(dve.tensor_tensor(window.rearrange("p (b t k) -> p b t k", b=DEC_B, t=DEC_T), taps_of(k),
                                           taps.unsqueeze(1).unsqueeze(1).to_broadcast([P, DEC_B, DEC_T, CONV_K]), ALU.mult), l)
                    link(dve.tensor_reduce(z[:, C_A + k, SEQ:T], window.rearrange("p (n k) -> p n k", k=CONV_K), AX.X, ALU.add), l)
                    if k == 1:
                        yield
                for k in range(4):
                    ins = dve.tensor_scalar(z[:, C_A + k, SEQ:T], z[:, C_A + k, SEQ:T], p("conv_b", k), None, ALU.add)
                ins.then_inc(E("conv_samples"), 1)
                yield
                first = chain[0]
                for tap in range(CONV_K):
                    for k in range(4):
                        src = hist_p[:, k, tap:tap + SEQ]
                        acc = z[:, C_A + k, 0:SEQ]
                        w = p("conv_w", k * CONV_K + tap)
                        if tap:
                            dve.wait_ge(dve_link, l * DVE_LINKS + before[k])
                            ins = dve.scalar_tensor_tensor(out=acc, in0=src, scalar=w, in1=acc, op0=ALU.mult, op1=ALU.add)
                        else:
                            if k == 0:
                                before = [0] * 4
                            ins = dve.tensor_scalar(acc, src, w, p("conv_b", k), ALU.mult, ALU.add)
                        if tap == CONV_K - 1 and k == 3:
                            ins.then_inc(E("conv_done"), 1)
                        else:
                            ins.then_inc(dve_link, 1)
                            chain[0] += 1
                            before[k] = chain[0]
                        if k % 2 == 1:
                            yield

            def layer_norm(l, l1, tile, mean_bank, var_bank, name):
                t4 = z[:, tile:tile + 4, :]
                dve.wait_ge(E(f"{name}_mean"), l1)
                dve.scalar_tensor_tensor(out=t4, in0=bcast(ps[:, mean_bank, 0:T], 4), scalar=-1.0 / 512, in1=t4,
                                         op0=ALU.mult, op1=ALU.add).then_inc(E(f"{name}_centred"), 1)
                yield
                dve.wait_ge(E(f"{name}_var"), l1)
                inverse(l, l1, ps[:, var_bank, 0:T], 512, rs[:, :], f"{name}_inv", 1e-5)
                yield
                dve.wait_ge(E(f"{name}_rstd"), l1)
                dve.tensor_tensor(t4, t4, bcast(rs[:, :], 4), ALU.mult).then_inc(E(f"{name}_scaled"), 1)

            def softmax_in(l, l1, cols, event):
                link(dve.tensor_tensor(small[:, 0, cols], small[:, 0, cols], p("sink", 0, 18)[:, cols], ALU.max), l)
                dve.tensor_scalar(small[:, 1, cols], small[:, 0, cols], -1.0, None, ALU.mult)
                dve.tensor_tensor(small[:, 2, cols], p("sink", 0, 18)[:, cols], small[:, 0, cols], ALU.subtract)\
                    .then_inc(E(event), 1)

            def softmax_out(l, l1, cols, probs, event):
                link(dve.tensor_tensor(small[:, 3, cols], small[:, 3, cols], small[:, 2, cols], ALU.add), l)
                link(dve.reciprocal(small[:, 4, cols], small[:, 3, cols]), l)
                n, m = probs.shape[1], probs.shape[2]
                dve.tensor_tensor(probs, probs, small[:, 4, cols].unsqueeze(2).to_broadcast([P, n, m]), ALU.mult)\
                    .then_inc(E(event), 1)

            def mixers(l, l1):
                dve.wait_ge(E("qk_sums"), l1)
                inverse(l, l1, ps[:, 2:7, 0:T], HD, r5, "qk_inv", 1e-6)
                yield
                dve.wait_ge(E("qk_rstd"), l1)
                dve.scalar_tensor_tensor(out=z[:, D_Q:D_Q + 4, :], in0=z[:, D_Q:D_Q + 4, :], scalar=p("q_g"), in1=r5[:, 0:4, :],
                                         op0=ALU.mult, op1=ALU.mult)
                dve.scalar_tensor_tensor(out=z[:, D_K, :], in0=z[:, D_K, :], scalar=p("k_g"), in1=r5[:, 4, :],
                                         op0=ALU.mult, op1=ALU.mult).then_inc(E("qk_normed"), 1)
                yield
                dve.wait_ge(E("qk_turned"), l1)
                link(dve.tensor_tensor(r5, ps[:, 2:7, 0:T], bcast(c("sin", T), 5), ALU.mult), l)
                dve.wait_ge(E("qk_normed"), l1)
                link(dve.tensor_tensor(z[:, D_Q:D_Q + 5, :], z[:, D_Q:D_Q + 5, :], bcast(c("cos", T), 5), ALU.mult), l)
                dve.tensor_tensor(z[:, D_Q:D_Q + 5, :], z[:, D_Q:D_Q + 5, :], r5, ALU.add).then_inc(E("qk_done"), 1)
                yield
                dve.wait_ge(E("scores0"), l1)
                link(dve.scalar_tensor_tensor(out=prob0, in0=ps[:, 2:4, :].rearrange("p a (h k) -> p (a h) k", k=P),
                                              scalar=HD ** -0.5, in1=bcast(c("band", P, P), 8), op0=ALU.mult, op1=ALU.add), l)
                link(dve.tensor_reduce(small[:, 0, 0:8], prob0, AX.X, ALU.max), l)
                softmax_in(l, l1, slice(0, 8), "shift0")
                yield
                dve.wait_ge(E("scores1"), l1)
                link(dve.scalar_tensor_tensor(out=prob1, in0=ps[:, 4:8, :].rearrange("p a (h k) -> p (a h) k", k=2 * P),
                                              scalar=HD ** -0.5, in1=bcast(c("band", 2 * P), 8), op0=ALU.mult, op1=ALU.add), l)
                link(dve.tensor_reduce(small[:, 0, 8:16], prob1, AX.X, ALU.max), l)
                softmax_in(l, l1, slice(8, 16), "shift1")
                yield
                dve.wait_ge(E("exp0"), l1)
                softmax_out(l, l1, slice(0, 8), prob0, "probs0")
                yield
                dve.wait_ge(E("exp1"), l1)
                softmax_out(l, l1, slice(8, 16), prob1, "probs1")
                yield
                yield
                dve.wait_ge(E("probs1_turned"), l1)
                dve.wait_ge(E("smp_hist"), l1)
                own = c("own", DEC_B).unsqueeze(2).to_broadcast([P, DEC_B, P])
                for kvh in range(2):
                    ins = dve.scalar_tensor_tensor(
                        out=prob_s[:, kvh, 0:1024].rearrange("p (b s) -> p b s", b=DEC_B),
                        in0=ps[:, 4 + 2 * kvh:6 + 2 * kvh, :].rearrange("p a (b s) -> p (a b) s", s=P),
                        scalar=HD ** -0.5, in1=own, op0=ALU.mult, op1=ALU.add)
                link(ins, l)
                for kvh in range(2):
                    v = prob_s[:, kvh, 0:1024].rearrange("p (b s) -> p b s", b=DEC_B)
                    dve.tensor_tensor(v, v, bcast(c("later"), DEC_B), ALU.add)
                yield
                dve.wait_ge(E("smp_new"), l1)
                link(dve.scalar_tensor_tensor(out=prob_s[:, :, 1024:1056], in0=ps[:, 2:4, 0:TS], scalar=HD ** -0.5,
                                              in1=bcast(c("new", TS), 2), op0=ALU.mult, op1=ALU.add), l)
                link(dve.tensor_reduce(small[:, 0, 16:18], prob_s, AX.X, ALU.max), l)
                softmax_in(l, l1, slice(16, 18), "shift_s")
                yield
                dve.wait_ge(E("exp_s"), l1)
                softmax_out(l, l1, slice(16, 18), prob_s, "probs_s")
                yield
                yield
                dve.wait_ge(E("decay_y"), l1)
                link(dve.tensor_scalar(bcum, e_last, 0.0, None, ALU.min), l)
                dve.wait_ge(E("decay_log"), l1)
                link(dve.tensor_tensor(bcum, bcum, e_pos, ALU.subtract), l)
                for k in range(2):
                    ins = dve.tensor_tensor_scan(e_last[:, k, :], c("seg", T), bcum[:, k, :], 0.0, ALU.mult, ALU.add)
                link(ins, l)
                dve.tensor_copy(bcum, e_last).then_inc(E("decay_sum"), 1)
                dve.wait_ge(E("decay_sum"), l1)
                for k in range(2):
                    v, w = e_last[:, k, 0:SEQ].rearrange("p (n i) -> p n i", i=64), bcum[:, k, 0:SEQ].rearrange("p (n i) -> p n i", i=64)
                    dve.tensor_tensor(v, w[:, :, 63:64].to_broadcast([P, NSEG, 64]), w, ALU.subtract)
                    v, w = e_last[:, k, SEQ:T].rearrange("p (n i) -> p n i", i=DEC_T), bcum[:, k, SEQ:T].rearrange("p (n i) -> p n i", i=DEC_T)
                    ins = dve.tensor_tensor(v, w[:, :, DEC_T - 1:DEC_T].to_broadcast([P, DEC_B, DEC_T]), w, ALU.subtract)
                ins.then_inc(E("last_diff"), 1)
                yield
                dve.wait_ge(E("e_pos_done"), l1)
                for par in range(2):
                    r = slice(64 * par, 64 * par + 64)
                    dve.scalar_tensor_tensor(out=qz[r, par:4:2, :], in0=z[r, A_Q:A_Q + 2, :], scalar=64 ** -0.5, in1=e_pos[r, :, :],
                                             op0=ALU.mult, op1=ALU.mult)
                dve.wait_ge(E("e_neg_done"), l1)
                dve.tensor_tensor(k_neg, z[:, A_K:A_K + 2, :], k_neg, ALU.mult).then_inc(E("k_neg_done"), 1)
                dve.wait_ge(E("e_last_done"), l1)
                dve.wait_ge(E("k_neg_done"), l1)
                dve.tensor_tensor(z[:, A_K:A_K + 2, :], z[:, A_K:A_K + 2, :], e_last, ALU.mult).then_inc(E("k_last_done"), 1)
                yield
                dve.wait_ge(E("att_in"), l1)
                for par in range(2):
                    for odd in range(2):
                        r = slice(64 * odd, 64 * odd + 64)
                        for hp in range(2):
                            dve.tensor_tensor(attz[r, 2 * hp + par, :, 64 * odd:64 * odd + 64],
                                              ps[r, 4 + par, hp * P:(hp + 1) * P].rearrange("p (a i) -> p a i", a=2),
                                              c("gla", 64)[r].unsqueeze(1).to_broadcast([64, 2, 64]), ALU.mult)
                    ins = dve.tensor_tensor(att_s[0:TS, par:4:2, :], ps[0:TS, 4 + par, 256:256 + 2 * TS].rearrange("p (h i) -> p h i", h=2),
                                            c("gla_s", TS)[0:TS].unsqueeze(1).to_broadcast([TS, 2, TS]), ALU.mult)
                ins.then_inc(E("att_done"), 1)
                dve.wait_ge(E("k_copied"), l1)
                dve.tensor_tensor(k_own[0:TS, :, :], k_tok_s[0:TS].unsqueeze(1).to_broadcast([TS, DEC_B, 2 * P]),
                                  c("of_b", DEC_B)[0:TS].unsqueeze(2).to_broadcast([TS, DEC_B, 2 * P]), ALU.mult)\
                    .then_inc(E("k_own_done"), 1)
                yield
                for ch in range(NSEG):
                    dve.wait_ge(E("update"), l * NSEG + ch + 1)
                    if ch >= 1:
                        dve.wait_ge(E("chunk_out"), l * NSEG + ch + 1)
                    for k in range(2):
                        for par in range(2):
                            r = slice(64 * par, 64 * par + 64)
                            u = ps[r, 4 + ch % 2, k * 256 + par * P:k * 256 + par * P + P]
                            if ch == 0:
                                ins = dve.tensor_copy(state[r, k, :], u)
                            else:
                                ins = dve.scalar_tensor_tensor(out=state[r, k, :], in0=state[r, k, :],
                                                               scalar=e_pos[r, k, ch * 64 + 63:ch * 64 + 64], in1=u,
                                                               op0=ALU.mult, op1=ALU.add)
                    ins.then_inc(E("state_done") if ch == NSEG - 1 else E("state_step"), 1)
                    if ch < NSEG - 1:
                        dve.wait_ge(E("state_step"), l * NSEG + ch + 1)
                    yield
                dve.wait_ge(E("state_done"), l1)
                dve.nop().then_inc(E("state_step"), 1)
                dve.wait_ge(E("smp_out"), l1)
                last = e_pos[:, :, SEQ:T].rearrange("p a (b t) -> p b a t", t=DEC_T)[:, :, :, DEC_T - 1:DEC_T]
                for k in range(2):
                    ins = dve.tensor_tensor(s_smp[:, :, k, :], s_smp[:, :, k, :], last[:, :, k, :].to_broadcast([P, DEC_B, P]), ALU.mult)
                link(ins, l)
                for b in range(DEC_B):
                    dve.wait_ge(E("smp_update"), l * DEC_B + b + 1)
                    for par in range(2):
                        r = slice(64 * par, 64 * par + 64)
                        u = ps[r, 4 + b % 2, :].rearrange("p (k n) -> p k n", k=2)[:, :, par * P:par * P + P]
                        ins = dve.tensor_tensor(s_smp[r, b, :, :], s_smp[r, b, :, :], u, ALU.add)
                    ins.then_inc(E("smp_added"), 1)
                    if b % 2:
                        yield
                dve.wait_ge(E("smp_added"), l * DEC_B + DEC_B)
                dve.nop().then_inc(E("state_s_done"), 1)
                dve.wait_ge(E("gla_sums"), l1)
                for h in range(4):
                    ins = dve.tensor_scalar(g_tmp[:, h, :], ps[:, (2, 3, 6, 7)[h], 0:T], 1.0 / P, 1e-6, ALU.mult, ALU.add)
                link(ins, l)
                dve.reciprocal(g_tmp, g_tmp).then_inc(E("gla_inv"), 1)
                yield
                dve.wait_ge(E("gla_rstd"), l1)
                link(dve.scalar_tensor_tensor(out=g_tmp, in0=gla_o, scalar=p("gla_g"), in1=g_tmp, op0=ALU.mult, op1=ALU.mult), l)
                dve.wait_ge(E("r_silu"), l1)
                dve.tensor_tensor(z[:, A_R:A_R + 4, :], z[:, A_R:A_R + 4, :], g_tmp, ALU.mult).then_inc(E("a_out"), 1)
                yield
                for _ in layer_norm(l, l1, B_V, 4, 5, "gm"):
                    yield
                yield
                dve.wait_ge(E("corner"), l1)
                dve.tensor_tensor(w_bd[0:TS, :, :].rearrange("p g (b t) -> p g b t", t=DEC_T),
                                  ps[0:TS, 7, 0:4 * DEC_T].rearrange("p (g t) -> p g t", g=4).unsqueeze(2).to_broadcast([TS, 4, DEC_B, DEC_T]),
                                  c("of_b", DEC_B)[0:TS].unsqueeze(1).unsqueeze(3).to_broadcast([TS, 4, DEC_B, DEC_T]), ALU.mult)\
                    .then_inc(E("w_bd_done"), 1)
                yield
                dve.wait_ge(E("mixed"), l1)
                for a in range(2):
                    ins = dve.tensor_tensor(g_tmp[:, :, a * P:(a + 1) * P], ps[:, 4 + a, :].rearrange("p (g t) -> p g t", g=4), b_sp[:, :, :], ALU.add)
                for g in range(4):
                    ins = dve.tensor_tensor(g_tmp[:, g, SEQ:T].rearrange("p (b t) -> p b t", t=DEC_T),
                                            ps[:, 7, g * TS:g * TS + TS].rearrange("p (b t) -> p b t", t=DEC_T),
                                            bcast(b_sp[:, g, 0:DEC_T], DEC_B), ALU.add)
                link(ins, l)
                dve.wait_ge(E("u_gelu"), l1)
                dve.tensor_tensor(z[:, B_U:B_U + 4, :], z[:, B_U:B_U + 4, :], g_tmp, ALU.mult).then_inc(E("b_out"), 1)
                yield

            dve.nop().then_inc(lo_dve, RING)
            dve.nop().then_inc(blocks_done, RING)
            dve.nop().then_inc(bank_free[0], 1)
            dve.nop().then_inc(bank_free[1], 1)
            dve.nop().then_inc(hid_free, 2)
            dve.memset(qz[:, :, :], 0.0)
            dve.memset(attz[:, :, :, :], 0.0)
            dve.memset(hist_p[:, :, 0:HIST], 0.0).then_inc(zeroed, 1)
            dve.wait_ge(zeroed, 1)
            dve.wait_ge(x_in, 16)
            dve.wait_ge(const_in, 16)
            with dve.Fori(0, DEPTH) as l:
                chain[0] = 0
                l1 = dve.snap(l + 1)
                dve.wait_ge(prm_in, l1 * 80)
                norm(l, l1, 1, 0)
                dve.wait_ge(E("lr_sums"), l1)
                dve.tensor_scalar(lr[0:16, :], ps[0:16, 6, 0:T], p("b_lr")[0:16], None, ALU.add).then_inc(E("lr_ready"), 1)
                conv_steps, mix = conv(l, l1), mixers(l, l1)
                for _ in range(CONV_AHEAD):
                    next(conv_steps, None)
                for _ in mix:
                    for _ in range(CONV_BETWEEN):
                        next(conv_steps, None)
                for _ in conv_steps:
                    pass
                for _ in layer_norm(l, l1, C_A, 2, 3, "cv"):
                    pass
                for b in range(BR0, BR0 + 3):
                    split(l, b)
                branch_in = ((A_R, "a_out"), (B_U, "b_out"), (C_A, "c_out"), (D_Q, "smp_od"))
                for i in range(4):
                    tile, event = branch_in[i]
                    dve.wait_ge(E(event), l1)
                    for k in range(4):
                        input_part(l, KC + 4 * i + k, z[:, tile + k, :])
                    if i >= 1:
                        branch_blocks(dve, split, l, i - 1)
                branch_blocks(dve, split, l, 3)
                for k in range(KC):
                    input_part(l, 3 * KC + k, gate[:, k, :])
                for t in range(KC):
                    split(l, O0 + t + 3)
                    dve.wait_ge(blocks_done, block_done_at(l, O0 + t))
                    dve.tensor_tensor(x[:, t, :], ps[:, t % 2, 0:T], x[:, t, :], ALU.add).then_inc(bank_free[t % 2], 1)
                dve.wait_ge(stored, l1 * (16 * STORES_PER_LAYER))
                dve.wait_ge(cached, l1 * 32)
                norm(l, l1, 2, 4 * KC)
                dve.wait_ge(xn_done, l * (2 * KC) + 2 * KC)
                dve.nop().then_inc(E("layer_free"), 1)
                with dve.Fori(0, 2 * HC // RING) as i:
                    n = dve.snap(i * RING)
                    for s in range(RING):
                        split(l, U0 + s + 3, n)
                        if s % 2:
                            k = s // 2
                            dve.wait_ge(bank_free[0], l * PER_BANK + ((TU + s - 1) // 2 + 2) + i * 2)
                            dve.wait_ge(blocks_done, block_done_at(l, U0 + s) + n)
                            dve.tensor_tensor(hidden[:, k, :], ps[:, 1, 0:T], gate_s[:, k, :], ALU.mult).then_inc(bank_free[1], 1)
                            dve.wait_ge(hid_hi, l * HC + (k + 1) + i * 2)
                            o = bass.ds(i * 2 + k, 1)
                            dve.tensor_tensor(h_lo[:, o, :], hidden[:, k:k + 1, :], h_hi[:, o, :].bitcast(f32), ALU.subtract)\
                                .then_inc(hid_lo, 1)
                            dve.nop().then_inc(hid_free, 1)
                for t in range(KC):
                    for q in range(3):
                        b = DN0 + 3 * t + q + 3
                        if b < BLOCKS:
                            split(l, b)
                    dve.wait_ge(blocks_done, block_done_at(l, DN0 + 3 * t + 2))
                    dve.tensor_tensor(x[:, t, :], ps[:, t % 2, 0:T], x[:, t, :], ALU.add).then_inc(bank_free[t % 2], 1)
                assert chain[0] == DVE_LINKS, chain[0]

        @block.gpsimd
        def _(pool):
            pool.wait_ge(const_in, 16)
            with pool.Fori(0, DEPTH) as l:
                l1 = pool.snap(l + 1)
                pool.wait_ge(prm_in, l1 * 80)
                pool.tensor_tensor(w_sp[:, :, :], w_sp[:, :, :], c("upper").unsqueeze(1).to_broadcast([P, 4, P]), ALU.mult)\
                    .then_inc(E("w_sp_masked"), 1)
                for b in range(POOL_BLOCKS):
                    s = b % RING
                    pool.wait_ge(hi_done, l * BLOCKS + (b + 1))
                    pool.tensor_tensor(w_lo[:, s, :], raw[:, s, :], w_hi[:, s, :].bitcast(f32), ALU.subtract).then_inc(lo_pool, 1)
                for i in range(1, 4):
                    for d in range(KC):
                        t = i * KC + d
                        pool.wait_ge(bank_free[t % 2], drained_at(l, TB + t))
                        if i >= 2:
                            pool.wait_ge(summed, l * (3 * KC) + (i - 2) * KC + d + 1)
                        pool.tensor_tensor(gate[:, d, :], gate[:, d, :], gate[:, t, :], ALU.add).then_inc(summed, 1)


def k_slot(k):
    if KC <= k < 3 * KC:
        i, u = (k - KC) // 4, (k - KC) % 4
        return 4 * (i % 2) + u
    return k % KC


def constants():
    t = np.zeros((P, CONSTS), np.float32)

    def put(name, a):
        t[0:a.shape[0], CONST_AT[name]:CONST_AT[name] + a.shape[1]] = a

    i = np.arange(P)
    put("ones", np.ones((P, P)))
    put("heads", i[:, None] // HD == i[None, :] // HD)
    half, rope = HD // 8, HD // 4
    turn = np.zeros((P, P))
    for h in (0, HD):
        for k in range(half):
            turn[h + half + k, h + k] = -1.0
            turn[h + k, h + half + k] = 1.0
    put("turn", turn)
    put("ident", np.eye(P))
    put("upper", i[:, None] <= i[None, :])
    d = i[:, None] - (np.arange(2 * P)[None, :] - P)
    put("band", np.where((d >= 0) & (d < WIN), 0.0, NEG))
    row_b, row_t = (i % TS) // DEC_T, i % DEC_T
    s, b = np.arange(TS), np.arange(DEC_B)
    put("own", np.where(row_b[:, None] == b[None, :], 0.0, NEG))
    put("later", np.where(i[None, :] > row_t[:, None], 0.0, NEG))
    put("new", np.where((s[None, :] // DEC_T == row_b[:, None]) & (s[None, :] % DEC_T <= row_t[:, None]), 0.0, NEG))
    tok = np.arange(T)
    first = np.where(tok < SEQ, tok % 64 == 0, tok % DEC_T == 0)
    put("seg", np.repeat(1.0 - first[None, :], P, 0))
    pos = np.where(tok < SEQ, tok, PAST + (tok - SEQ) % DEC_T).astype(np.float32)
    inv = np.exp(np.float32(-math.log(500000.0)) * np.arange(half, dtype=np.float32) * np.float32(2.0 / rope))
    ang = (pos[None, :] * inv[:, None]).astype(np.float32)
    cos, sin = np.ones((P, T)), np.zeros((P, T))
    for h in (0, HD):
        for k in (0, half):
            cos[h + k:h + k + half], sin[h + k:h + k + half] = np.cos(ang), np.sin(ang)
    put("cos", cos)
    put("sin", sin)
    put("gla", (i[:, None] % 64) <= np.arange(64)[None, :])
    put("gla_s", (s[:, None] // DEC_T == s[None, :] // DEC_T) & (s[:, None] <= s[None, :]))
    put("of_b", s[:, None] // DEC_T == b[None, :])
    put("rep", np.arange(P)[:, None] == s[None, :] % DEC_T)
    return t


def kernel(**inputs):
    import concourse.bacc as bacc
    from concourse.bass_utils import run_bass_kernel_spmd

    a = {k: np.asarray(v) for k, v in inputs.items()}
    L = DEPTH

    def per_feature(v):
        return v.reshape(L, -1, P).transpose(0, 2, 1)

    def blocks(w):
        k, n = w.shape[1] // P, w.shape[2] // P
        return np.ascontiguousarray(w.reshape(L, k, P, n, P).transpose(0, 3, 2, 1, 4)).reshape(L * n, P, k * P)

    heads = np.arange(8).reshape(2, 4).T.reshape(-1)
    q_cols = (heads[:, None] * HD + np.arange(HD)[None, :]).reshape(-1)
    span = lambda at, n: np.arange(at, at + n)
    cols = np.concatenate([span(2576, 512), span(3088, 512), 3600 + q_cols, span(4112, 128), span(4240, 128),
                           span(0, 256), span(256, 256), span(512, 512), span(1024, 512), span(1552, 512),
                           span(2064, 512)])
    w_in, w_br = a["w_in"], a["w_branch"]
    w_br3 = w_br[:, 3][:, q_cols]
    w_b = np.concatenate([w_br[:, 0:3], w_br3[:, None]], 1)
    w_b = w_b.reshape(L, 4, 4, P, 4, 2, P).transpose(0, 1, 4, 3, 5, 2, 6)
    up = a["w_gate_up"].reshape(L, D_MODEL, 2, HC, P).transpose(0, 1, 3, 2, 4).reshape(L, D_MODEL, 2 * FFN)
    sink = a["sinks"]
    sink_p = np.broadcast_to(sink[:, None, :], (L, P, 8))
    sink_s = np.repeat(sink.reshape(L, 2, 4).transpose(0, 2, 1), TS, 1)
    b_lr = np.zeros((L, P, 1), np.float32)
    b_lr[:, 0:16, 0] = a["b_in"][:, 1536:1552]
    params = np.concatenate([
        per_feature(a["b_in"][:, cols]), per_feature(a["b_gate"]), per_feature(a["norm1_g"]), per_feature(a["norm2_g"]),
        per_feature(a["b_alpha"]), per_feature(a["gla_norm_g"]), per_feature(a["gmlp_ln_g"]), per_feature(a["gmlp_ln_b"]),
        a["conv_w"].reshape(L, CONV_K, 4, P).transpose(0, 3, 2, 1).reshape(L, P, 4 * CONV_K), per_feature(a["conv_b"]),
        per_feature(a["conv_ln_g"]), per_feature(a["conv_ln_b"]),
        np.concatenate([a["q_norm_g"]] * 2, 1)[:, :, None], np.concatenate([a["k_norm_g"]] * 2, 1)[:, :, None],
        sink_p, sink_p, sink_s, b_lr], 2)
    xs = np.concatenate([a["x_prompt"].reshape(SEQ, D_MODEL), a["x_sample"].reshape(TS, D_MODEL)], 0)
    arrays = {
        "x": xs.reshape(T, KC, P).transpose(2, 1, 0).reshape(P, KC * T),
        "consts": constants(),
        "params": params,
        "w_lr": w_in[:, :, 1536:1552].reshape(L, KC, P, 16).transpose(0, 2, 1, 3).reshape(L, P, KC * 16),
        "w_z": blocks(w_in[:, :, cols]),
        "w_gate": blocks(a["w_gate"]),
        "w_branch": w_b.reshape(L * 16, P, 1024),
        "w_out": blocks(a["w_out"]),
        "w_up": blocks(up),
        "w_down": blocks(a["w_down"]),
        "w_a2": a["w_alpha2"],
        "w_sp": a["w_spatial"].transpose(0, 3, 1, 2).reshape(L, P, 4 * P),
        "b_sp": np.broadcast_to(a["b_spatial"].reshape(L, 1, 4 * P), (L, P, 4 * P)),
        "conv_hist": a["state_conv"].reshape(L, DEC_B, HIST, 4, P).transpose(0, 4, 3, 1, 2).reshape(L, P, -1),
        "k_hist": a["cache_swa_k"].reshape(L, DEC_B, WIN, P).transpose(0, 3, 1, 2).reshape(L, P, -1),
        "v_hist": a["cache_swa_v"].reshape(L, DEC_B, WIN, P).transpose(0, 2, 1, 3).reshape(L, P, -1),
        "cache_k": a["cache_swa_k"].reshape(L, DEC_B, WIN, P),
        "cache_v": a["cache_swa_v"].reshape(L, DEC_B, WIN, P),
        "state": a["state_gla"].reshape(L, DEC_B, 2, P, 128).transpose(0, 3, 1, 2, 4).reshape(L, P, -1),
    }
    arrays = {k: np.ascontiguousarray(v) for k, v in arrays.items()}
    outs = {
        "y": (P, KC * T), "gmlp_v": (L, P, 4 * TS), "gla_prompt": (L, P, 2 * P), "gla_sample": (L, P, 2048),
        "conv_prompt": (L, P, 4 * HIST), "conv_sample": (L, P, 4 * DEC_B * EXT), "k_prompt": (L, P, WIN),
        "v_prompt": (L, P, WIN), "k_sample": (L, DEC_B, WIN, P), "v_sample": (L, DEC_B, WIN, P)}
    nc = bacc.Bacc("TRN2", target_bir_lowering=False, num_devices=1, dynamic_dma_scratch_size=1024)
    dram = {}
    for name, v in arrays.items():
        dram[name] = nc.dram_tensor(f"in_{name}", v.shape, mybir.dt.from_np(v.dtype), kind="ExternalInput").ap()
    for name, shape in outs.items():
        dram[name] = nc.dram_tensor(f"out_{name}", shape, mybir.dt.float32, kind="ExternalOutput").ap()
    trunk_program(nc, dram)
    r = run_bass_kernel_spmd(nc, [{f"in_{k}": v for k, v in arrays.items()}], core_ids=[0]).results[0]

    y = r["out_y"].reshape(P, KC, T).transpose(2, 1, 0).reshape(T, D_MODEL)
    gla_p = r["out_gla_prompt"].reshape(L, P, 2, 128).transpose(0, 2, 1, 3).reshape(L, 1, 4, 64, 128)
    gla_s = r["out_gla_sample"].reshape(L, P, DEC_B, 2, 128).transpose(0, 2, 3, 1, 4).reshape(L, DEC_B, 4, 64, 128)
    conv_p = r["out_conv_prompt"].reshape(L, P, 4, HIST).transpose(0, 3, 2, 1).reshape(L, 1, HIST, CONV_W)
    conv_s = r["out_conv_sample"].reshape(L, P, 4, DEC_B, EXT)[..., DEC_T:].transpose(0, 3, 4, 2, 1)\
        .reshape(L, DEC_B, HIST, CONV_W)
    token_rows = lambda v: v.transpose(0, 2, 1).reshape(L, 1, WIN, 2, HD)
    gm = r["out_gmlp_v"].reshape(L, P, 4, DEC_B, DEC_T).transpose(0, 3, 4, 2, 1).reshape(L, DEC_B, DEC_T, 512)
    out = (y[0:SEQ].reshape(1, SEQ, D_MODEL), y[SEQ:T].reshape(DEC_B, DEC_T, D_MODEL), gla_p, gla_s, conv_p, conv_s,
           token_rows(r["out_k_prompt"]), token_rows(r["out_v_prompt"]), r["out_k_sample"].reshape(L, DEC_B, WIN, 2, HD),
           r["out_v_sample"].reshape(L, DEC_B, WIN, 2, HD), gm)
    return tuple(np.ascontiguousarray(o) for o in out)
```

```python
import math
from contextlib import ExitStack

import concourse.bass as bass
import numpy as np
from concourse import mybir

DEPTH, D_MODEL, SEQ, DEC_B, DEC_T, PAST = 2, 1024, 256, 8, 4, 2048
WIN, HD, CONV_K, CONV_W = 128, 64, 31, 512
FFN = 2816
IN_COLS = 4368
P = 128
TS = DEC_B * DEC_T
T = SEQ + TS
KC = D_MODEL // P
HC = FFN // P
NSEG = SEQ // 64
HIST = CONV_K - 1
EXT = DEC_T + HIST
NEG = -1.0e30

C_A, C_G, D_Q, D_K, D_V, A_Q, A_K, A_V, A_R, B_U, B_V = 0, 4, 8, 12, 13, 14, 16, 18, 22, 26, 30
NZ = 34
HALVED = (D_K, D_V)

RING = 4
UNIT = P
SLOT = KC * UNIT
DOWN_UNITS = (6, 8, 8)
Z0 = 0
G0 = Z0 + NZ + len(HALVED)
BR0 = G0 + 4 * KC
O0 = BR0 + 2 * KC
U0 = O0 + KC
DN0 = U0 + 2 * HC
BLOCKS = DN0 + 3 * KC
TZ, TG = 0, NZ
TB = TG + 4 * KC
TO = TB + 4 * KC
TU = TO + KC
TD = TU + 2 * HC
TILES = TD + KC

POOL_BLOCKS = BR0 + RING
DVE_BLOCKS = BLOCKS - POOL_BLOCKS
PER_BANK = [TB // 2 + (TILES - TB) // 4] * 2 + [(TILES - TB) // 4] * 2
assert TB % 2 == 0 and (TILES - TB) % 4 == 0 and (TU - TB) % 4 == 0
assert BLOCKS % RING == 0 and G0 % RING == 0 and U0 % RING == 0 and DN0 % RING == 0 and TILES % 2 == 0

_cols, PARAM_AT = 0, {}
for _name, _n in (("b_in", NZ), ("b_gate", 4 * KC), ("norm1", KC), ("norm2", KC), ("b_alpha", 2), ("gla_g", 1),
                  ("gmlp_g", 4), ("gmlp_b", 4), ("conv_w", 4 * CONV_K), ("conv_b", 4), ("conv_g", 4),
                  ("conv_lb", 4), ("q_g", 1), ("k_g", 1), ("sink", 18), ("b_lr", 1)):
    PARAM_AT[_name] = _cols
    _cols += _n
PARAMS = _cols
CONST_AT, _cols = {}, 0
for _name, _n in (("ones", P), ("heads", P), ("turn", P), ("ident", P), ("upper", P), ("band", 2 * P),
                  ("own", DEC_B), ("later", P), ("new", TS), ("eps6", 1), ("eps5", 1), ("seg", T), ("cos", T), ("sin", T),
                  ("gla", 64), ("gla_s", TS), ("of_b", DEC_B), ("rep", TS)):
    CONST_AT[_name] = _cols
    _cols += _n
CONSTS = _cols

STEP = dict(
    n1_sums=3, n1_rstd=4, c_gate=9, qk_sq=19, qk_sums=19, qk_rstd=20, qk_turned=21, scores0=23, tok_copied=23,
    scores1=24, exp0=26, exp1=28, probs_turned=29, probs_copied=29, prompt_pv=30, prompt_od=30, smp_new=31,
    exp_s=34, probs_s_turned=36, probs_s_copied=37, smp_pv=38, smp_od=38, decay_in=37, decay_log=39,
    v_copied=38, decay_exp=40, att_in=42, k_copied=43, gelu=44, chunks=44, smp_old=46, old_out=47, smp_out=48,
    gla_o=49, cv_mean=50, cv_sq=50, smp_update=50, gla_sums=53, gla_rstd=54, cv_var=53, r_silu=55, c_silu=56,
    a_parts=56, gates0=58, gm_mean=60, gm_sq=61, gm_var=62, gv_done=63, gv_turned=64, gv_copied=67, mixed=68,
    gates1=60, gates2=69, gates3=74, gm_add=0, gm_centre=0, gm_add2=0, gm_scale=0, w_bd=0, b_out=68, in1=69,
    in2=70, in3=78, scale2=68, scale3=72)

CONV_AHEAD, CONV_BETWEEN = 9, 2
DVE_LINKS = 163
ACT_LINKS = 8
STORES_PER_LAYER = 9

ORDER = (0, 3, 2, 1)
BRANCH_IN = ((A_R, "a_out"), (D_Q, "smp_od"), (C_A, "c_out"), (B_U, "b_out"))
SPLIT_STEPS = {"in1": 1, "in2": 2, "in3": 3}


def bank_of(t):
    return t % 2 if t < TB else (t - TB) % 4


def turn_of(t):
    return t // 2 if t < TB else (t - TB) // 4 + (TB // 2 if bank_of(t) < 2 else 0)


def z_blocks():
    for t in range(NZ):
        if t in HALVED:
            yield t, 0, 4
            yield t, 4, 4
        else:
            yield t, 0, 8


def trunk_program(nc, dram):
    f32, f32r = mybir.dt.float32, mybir.dt.float32r
    ACT, ALU, AX = mybir.ActivationFunctionType, mybir.AluOpType, mybir.AxisListType
    ctx = ExitStack()
    with ctx:
        def sb(name, cols, dt=f32):
            return ctx.enter_context(nc.sbuf_tensor(name, [P, *cols], dt))

        def sem(name):
            return ctx.enter_context(nc.semaphore(name))

        over_at = -(-nc.sbuf_base // 32) * 32
        sb("over", [(NZ + 4 * KC) * T + 8])
        zg = nc.alloc_sbuf_tensor_at("zg", [P, NZ + 4 * KC, T], f32, offset=over_at)
        h_hi = nc.alloc_sbuf_tensor_at("h_hi", [P, HC, T], f32r, offset=over_at)
        h_lo = nc.alloc_sbuf_tensor_at("h_lo", [P, HC, T], f32r, offset=over_at + 4 * HC * T)

        zg_r = nc.alloc_sbuf_tensor_at("zg_r", [P, NZ + 4 * KC, T], f32r, offset=over_at)
        a_hi, a_lo = zg_r[:, C_G:C_G + 4, :], zg_r[:, A_V:A_V + 4, :]
        m_hi, m_lo = zg_r[:, 2 * HC:2 * HC + KC, :], zg_r[:, 2 * HC + KC:2 * HC + 2 * KC, :]

        raw = sb("raw", [RING, SLOT])
        w_hi, w_lo = sb("w_hi", [RING, SLOT], f32r), sb("w_lo", [RING, SLOT], f32r)
        x = sb("x", [KC, T])
        x_hi, x_lo = sb("x_hi", [KC, T], f32r), sb("x_lo", [KC, T], f32r)
        z, gate = zg[:, 0:NZ, :], zg[:, NZ:NZ + 4 * KC, :]
        work = sb("work", [6144])
        kv = sb("kv", [2048])
        prm = sb("prm", [PARAMS])
        cst = sb("cst", [CONSTS])
        w_lr = sb("w_lr", [KC, 16])
        w_a2 = sb("w_a2", [2 * P])
        w_sp = sb("w_sp", [4, P])
        b_sp = sb("b_sp", [4, P])
        w_bd = sb("w_bd", [4, TS])
        hist_p = sb("hist_p", [4, SEQ + HIST])
        hist_s = sb("hist_s", [4, DEC_B, EXT])
        qz = sb("qz", [4, T])
        attz = sb("attz", [4, 2, P])
        vt = sb("vt", [2, P])
        vs = sb("vs", [2, P])
        small = sb("small", [5, 18])
        rs = sb("rs", [T])
        lr = sb("lr", [T])
        rs_m = sb("rs_m", [T])
        q_smp = sb("q_smp", [P])
        state = sb("state", [2, P])
        ps = ctx.enter_context(nc.psum_tensor("ps", [P, 8, 512], f32))

        def p(name, i=0, n=1):
            at = PARAM_AT[name] + i
            return prm[:, at:at + n]

        def c(name, n=None, i=0):
            at = CONST_AT[name] + i
            return cst[:, at:at + (n or P)]

        added = work[:, 5760:5760 + T]
        sq = work[:, 0:KC * T].rearrange("p (c t) -> p c t", t=T)
        sq5 = work[:, 0:5 * T].rearrange("p (c t) -> p c t", t=T)
        r5 = work[:, 5 * T:10 * T].rearrange("p (c t) -> p c t", t=T)
        prob = work[:, 0:3072]
        prob_t = work[:, 3072:6144]
        prob0 = prob[:, 0:1024].rearrange("p (h k) -> p h k", k=P)
        prob1 = prob[:, 1024:3072].rearrange("p (h k) -> p h k", k=2 * P)
        prob_s = prob[:, 0:2 * 1056].rearrange("p (v k) -> p v k", k=1056)
        prob0_t = prob_t[:, 0:1024]
        prob1_t = prob_t[:, 1024:3072].rearrange("p (a n) -> p a n", a=2)
        prob_st = prob_t[:, 0:2048].rearrange("p (v b r) -> p v b r", v=2, b=DEC_B)
        prob_nt = prob_t[:, 2048:2048 + 2 * P].rearrange("p (v r) -> p v r", v=2)
        gl = work[:, 0:2304].rearrange("p (a c t) -> p a c t", a=4, t=T)
        bcum, e_pos, k_neg, e_last = gl[:, 0], gl[:, 1], gl[:, 2], gl[:, 3]
        v_tok = zg[:, C_G:C_G + 4, :].rearrange("p a t -> p (a t)")[:, 0:1024]\
            .rearrange("p (a n) -> p a n", a=2)
        v_tok_s = work[:, 2304:2816]
        k_tok = work[:, 2816:3328].rearrange("p (a n) -> p a n", a=2)
        k_tok_s = work[:, 3328:3584]
        att_s = work[:, 3584:3712].rearrange("p (h i) -> p h i", h=4)
        k_own = work[:, 3712:5760].rearrange("p (b n) -> p b n", b=DEC_B)
        q_own = work[:, 1152:1152 + DEC_B * P].rearrange("p (b n) -> p b n", b=DEC_B)
        old_out = work[:, 2176:2304]
        gla_o = z[:, A_Q:A_Q + 4, :]
        c_sq = z[:, C_G:C_G + 4, :]
        g_sq = work[:, 0:4 * T].rearrange("p (c t) -> p c t", t=T)
        g_tmp = work[:, 4 * T:8 * T].rearrange("p (c t) -> p c t", t=T)
        gv_tok = work[:, 2304:3328].rearrange("p (a n) -> p a n", a=2)
        gv_tok_s = work[:, 3328:3840]
        window = work[:, 3072:3072 + TS * CONV_K]
        gate_s = work[:, 2304:2304 + 2 * T].rearrange("p (a t) -> p a t", a=2)
        hidden = work[:, 2304 + 2 * T:2304 + 4 * T].rearrange("p (a t) -> p a t", a=2)

        def own_columns():
            a = q_own[:, 0, 0:DEC_T]
            return bass.AP(tensor=a.tensor, offset=a.offset, ap=[a.ap[0], [TS, 4], [P + DEC_T, DEC_B], [1, DEC_T]])

        def taps_of(k):
            a = hist_s[:, k, :, 0:DEC_T]
            return bass.AP(tensor=a.tensor, offset=a.offset, ap=[*a.ap, [1, CONV_K]])

        k_hist, v_hist = kv[:, 0:1024], kv[:, 1024:2048].rearrange("p (b n) -> p b n", b=DEC_B)
        s_smp = kv[:, :].rearrange("p (b a v) -> p b a v", b=DEC_B, a=2)

        raw_in = [sem(f"raw_in{s}") for s in range(RING)]
        hi_done = sem("hi_done")
        lo_pool = sem("lo_pool")
        lo_dve = sem("lo_dve")
        blocks_done = sem("blocks_done")
        bank_free = [sem(f"bank_free{i}") for i in range(4)]
        xh_done, xl_done = sem("xh_done"), sem("xl_done")
        sq_done = sem("sq_done")
        squares = sem("squares")
        silu_done, gate_ready = sem("silu_done"), sem("gate_ready")
        hid_hi, hid_lo = sem("hid_hi"), sem("hid_lo")
        summed = sem("summed")
        dve_link, act_link = sem("dve_link"), sem("act_link")
        x_in = [sem("x_in0"), sem("x_in1")]
        const_in, prm_in, w_lr_in, small_in, hist_in, kv_in, state_in = (
            sem(n) for n in ("const_in", "prm_in", "w_lr_in", "small_in", "hist_in", "kv_in", "state_in"))
        zeroed = sem("zeroed")
        stored, cached, y_out = sem("stored"), sem("cached"), sem("y_out")
        ev = {}

        def E(name):
            if name not in ev:
                ev[name] = sem(name)
            return ev[name]

        def steps_of(place):
            def at(step):
                while place[0] < STEP[step]:
                    yield
            return at

        def branch_part(k):
            if k < 4:
                return a_hi[:, k, :], a_lo[:, k, :]
            return x_hi[:, k_slot(KC + k), :], x_lo[:, k_slot(KC + k), :]

        block = ctx.enter_context(nc.Block())

        def block_done_at(l, b):
            return l * BLOCKS + (b + 1 + RING)

        def slot_free_at(l, b):
            return l * BLOCKS + (b + 1)

        def lo_dve_at(l, b):
            return l * DVE_BLOCKS + (b - POOL_BLOCKS + 1 + RING)

        def wait_lo(eng, l, b, dyn=0):
            if b < POOL_BLOCKS:
                eng.wait_ge(lo_pool, l * POOL_BLOCKS + (b + 1) + dyn)
            else:
                eng.wait_ge(lo_dve, lo_dve_at(l, b) + dyn)

        def wait_drained(eng, l, t, dyn=0):
            eng.wait_ge(bank_free[bank_of(t)], l * PER_BANK[bank_of(t)] + (turn_of(t) + 2) + dyn)

        def x_part_at(l, k):
            return l * (5 * KC) + (k + 1)

        def x_half(i):
            return dram["x"].rearrange("p (h c t) -> p h c t", h=2, t=T)[:, i]

        @block.sync
        def _(sp):
            def row(name, i):
                return dram[name][bass.ds(sp.snap(i), 1)].rearrange("a p n -> (a p) n")

            def load(src, b, l, dyn, units, layer_free=None):
                s = b % RING
                if b < RING:
                    sp.wait_ge(lo_dve, l * DVE_BLOCKS + (b + 1))
                else:
                    wait_lo(sp, l, b - RING, dyn)
                if layer_free is not None:
                    sp.wait_ge(E("layer_free"), layer_free)
                sp.dma_start(raw[:, s, 0:units * UNIT], src).then_inc(raw_in[s], 16)

            sp.dma_start(x[:, 0:KC // 2, :], x_half(0)).then_inc(x_in[0], 16)
            with sp.Fori(0, DEPTH) as l:
                l1 = sp.snap(l + 1)
                for b in range(RING):
                    load(row("w_z", l * NZ + b), b, l, 0, 8)
                    if b == 0:
                        sp.dma_start(prm[:, :], row("params", l)).then_inc(prm_in, 16)
                        sp.dma_start(w_lr[:, :, :], row("w_lr", l).rearrange("p (c n) -> p c n", n=16)).then_inc(w_lr_in, 16)
                for b, (t, u, n) in enumerate(z_blocks()):
                    if b >= RING:
                        load(row("w_z", l * NZ + t)[:, u * UNIT:(u + n) * UNIT], b, l, 0, n)
                    if b == 6:
                        sp.dma_start(hist_s[:, :, :, 0:HIST],
                                     row("conv_hist", l).rearrange("p (c b t) -> p c b t", c=4, b=DEC_B))\
                            .then_inc(hist_in, 16)
                    if b == 10:
                        sp.dma_start(w_a2[0:16, :], row("w_a2", l)).then_inc(small_in, 16)
                        sp.dma_start(w_sp[:, :, :], row("w_sp", l).rearrange("p (g t) -> p g t", g=4)).then_inc(small_in, 16)
                        sp.dma_start(b_sp[:, :, :], row("b_sp", l).rearrange("p (g t) -> p g t", g=4)).then_inc(small_in, 16)
                    if b == 14:
                        sp.dma_start(k_hist, row("k_hist", l)).then_inc(kv_in, 16)
                    if b == 18:
                        sp.dma_start(kv[:, 1024:2048], row("v_hist", l)).then_inc(kv_in, 16)
                    if b in (24, 30):
                        old, new = ("cache_k", "k_sample") if b == 24 else ("cache_v", "v_sample")
                        sp.dma_start(dram[new][bass.ds(l, 1)].rearrange("a b t n -> (a b) t n")[:, 0:WIN - DEC_T, :],
                                     dram[old][bass.ds(l, 1)].rearrange("a b t n -> (a b) t n")[:, DEC_T:WIN, :])\
                            .then_inc(cached, 16)
                for b in range(RING):
                    load(row("w_gate", l * 4 * KC + b), G0 + b, l, 0, 8)
                with sp.Fori(1, 4 * KC // RING) as i:
                    for s in range(RING):
                        n = sp.snap(l * 4 * KC + i * RING + s)
                        load(row("w_gate", n), G0 + s, l, i * RING, 8)
                for b in range(2 * KC):
                    load(row("w_branch", l * 2 * KC + b), BR0 + b, l, 0, 8)
                for b in range(KC):
                    load(row("w_out", l * KC + b), O0 + b, l, 0, 8)
                sp.wait_ge(E("gv_done"), l1)
                sp.dma_start(row("gmlp_v", l).rearrange("p (c t) -> p c t", c=4), z[:, B_V:B_V + 4, SEQ:T]).then_inc(stored, 16)
                sp.wait_ge(E("state_done"), l1)
                sp.dma_start(row("gla_prompt", l), state[:, :, :].rearrange("p a v -> p (a v)")).then_inc(stored, 16)
                sp.wait_ge(E("state_s_done"), l1)
                sp.dma_start(row("gla_sample", l), kv[:, :]).then_inc(stored, 16)
                sp.wait_ge(E("conv_h"), l1)
                sp.dma_start(row("conv_prompt", l).rearrange("p (c t) -> p c t", c=4), hist_p[:, :, SEQ:SEQ + HIST]).then_inc(stored, 16)
                sp.dma_start(row("conv_sample", l), hist_s[:, :, :, :].rearrange("p c b t -> p (c b t)")).then_inc(stored, 16)
                sp.wait_ge(E("qk_done"), l1)
                sp.dma_start(row("k_prompt", l), z[:, D_K, WIN:SEQ]).then_inc(stored, 16)
                sp.dma_start(row("v_prompt", l), z[:, D_V, WIN:SEQ]).then_inc(stored, 16)
                sp.wait_ge(E("tok_copied"), l1)
                for i, new in enumerate(("v_sample", "k_sample")):
                    sp.dma_start(dram[new][bass.ds(l, 1)].rearrange("a b t n -> (a b) t n")[:, WIN - DEC_T:WIN, :],
                                 vs[0:TS, i, :]).then_inc(stored, 16)
                with sp.Fori(0, 2 * HC // RING) as i:
                    for s in range(RING):
                        n = sp.snap(l * 2 * HC + i * RING + s)
                        load(row("w_up", n), U0 + s, l, i * RING, 8)
                for d in range(KC):
                    at = 0
                    for q, n in enumerate(DOWN_UNITS):
                        free = d == KC - 1 and q == 2
                        load(row("w_down", l * KC + d)[:, at * UNIT:(at + n) * UNIT], DN0 + 3 * d + q, l, 0, n,
                             l1 if free else None)
                        at += n
            for k in range(KC):
                wait_drained(sp, DEPTH - 1, TD + k)
                sp.dma_start(dram["y"][:, k * T:(k + 1) * T], x[:, k, :]).then_inc(y_out, 16)
            sp.wait_ge(y_out, 16 * KC)

        @block.tensor
        def _(pe):
            place = [0]
            at = steps_of(place)

            def split_mm(out, slot, u, rh, rl, start, stop):
                wh = w_hi[:, slot, u * UNIT:(u + 1) * UNIT]
                wl = w_lo[:, slot, u * UNIT:(u + 1) * UNIT]
                pe.matmul(out, wh, rh, start=start, stop=False)
                pe.matmul(out, wh, rl, start=False, stop=False)
                return pe.matmul(out, wl, rh, start=False, stop=stop)

            def bank_at_turn(l, t):
                return l * PER_BANK[bank_of(t)] + (turn_of(t) + 1)

            def bank_wait(l, t, dyn=0):
                pe.wait_ge(bank_free[bank_of(t)], bank_at_turn(l, t) + dyn)

            def sum_of(bank, src, event):
                pe.matmul(ps[:, bank, 0:T], c("ones"), src, start=True, stop=True).then_inc(E(event), 1)

            def mixers(l, l1):
                pe.wait_ge(E("w_lr_ready"), l1)
                for k in range(KC):
                    mm = pe.matmul(ps[0:16, 6, 0:T], w_lr[:, k, :], x[:, k, :], start=k == 0, stop=k == KC - 1)
                mm.then_inc(E("lr_sums"), 1)
                yield from at("n1_sums")
                pe.wait_ge(const_in, 16)
                pe.wait_ge(E("n1_added"), l1)
                sum_of(7, added, "n1_sums")
                yield from at("qk_sums")
                pe.wait_ge(E("qk_sq"), l1)
                pe.wait_ge(E("lr_ready"), l1)
                for k in range(5):
                    mm = pe.matmul(ps[:, 2 + k, 0:T], c("heads"), sq5[:, k, :], start=True, stop=True)
                mm.then_inc(E("qk_sums"), 1)
                yield from at("qk_turned")
                pe.wait_ge(E("qk_normed"), l1)
                for k in range(5):
                    mm = pe.matmul(ps[:, 2 + k, 0:T], c("turn"), z[:, D_Q + k, :], start=True, stop=True)
                mm.then_inc(E("qk_turned"), 1)
                yield from at("scores0")
                pe.wait_ge(E("qk_done"), l1)
                for k in range(2):
                    pe.transpose(ps[:, 7, k * P:(k + 1) * P], z[:, D_V, k * P:(k + 1) * P], c("ident"))
                pe.transpose(ps[0:TS, 7, 2 * P:3 * P], z[:, D_V, SEQ:T], c("ident"))
                pe.transpose(ps[0:TS, 7, 3 * P:4 * P], z[:, D_K, SEQ:T], c("ident")).then_inc(E("tok_turned"), 1)
                for kvh in range(2):
                    r = slice(64 * kvh, 64 * kvh + 64)
                    for j in range(4):
                        mm = pe.matmul(ps[:, 2 + kvh, j * P:(j + 1) * P], z[r, D_Q + j, 0:P], z[r, D_K, 0:P],
                                       start=True, stop=True)
                mm.then_inc(E("scores0"), 1)
                yield from at("scores1")
                pe.wait_ge(E("tok_copied"), l1)
                for kvh in range(2):
                    r = slice(64 * kvh, 64 * kvh + 64)
                    for j in range(4):
                        mm = pe.matmul(ps[:, 4 + 2 * kvh + j // 2, (j % 2) * 256:(j % 2) * 256 + 256],
                                       z[r, D_Q + j, P:SEQ], z[r, D_K, 0:SEQ], start=True, stop=True)
                mm.then_inc(E("scores1"), 1)
                yield from at("probs_turned")
                pe.wait_ge(E("probs0"), l1)
                for h in range(8):
                    mm = pe.transpose(ps[:, 2 + h // 4, (h % 4) * P:(h % 4 + 1) * P], prob0[:, h, :], c("ident"))
                mm.then_inc(E("probs0_turned"), 1)
                pe.wait_ge(E("probs1"), l1)
                for a in range(2):
                    for h in range(8):
                        mm = pe.transpose(ps[:, 4 + 2 * a + h // 4, (h % 4) * P:(h % 4 + 1) * P],
                                          prob1[:, h, a * P:(a + 1) * P], c("ident"))
                mm.then_inc(E("probs1_turned"), 1)
                yield from at("prompt_pv")
                pe.wait_ge(E("probs1_copied"), l1)
                for kvh in range(2):
                    r = slice(64 * kvh, 64 * kvh + 64)
                    pe.matmul(ps[r, 2, :], vt[:, 0, r], prob0_t[:, 512 * kvh:512 * kvh + 512], start=True, stop=True)
                    for a in range(2):
                        mm = pe.matmul(ps[r, 3, :], vt[:, a, r], prob1_t[:, a, 512 * kvh:512 * kvh + 512],
                                       start=a == 0, stop=a == 1)
                mm.then_inc(E("prompt_pv"), 1)
                pe.wait_ge(kv_in, l1 * 32)
                pe.wait_ge(E("q_smp"), l1)
                for kvh in range(2):
                    r = slice(64 * kvh, 64 * kvh + 64)
                    for half in range(2):
                        mm = pe.matmul(ps[:, 4 + 2 * kvh + half, :], q_smp[r, :], k_hist[r, half * 512:half * 512 + 512],
                                       start=True, stop=True)
                mm.then_inc(E("smp_hist"), 1)
                yield from at("smp_new")
                pe.wait_ge(E("prompt_od"), l1)
                for kvh in range(2):
                    r = slice(64 * kvh, 64 * kvh + 64)
                    mm = pe.matmul(ps[:, 2 + kvh, 0:TS], q_smp[r, :], z[r, D_K, SEQ:T], start=True, stop=True)
                mm.then_inc(E("smp_new"), 1)
                yield from at("probs_s_turned")
                pe.wait_ge(E("probs_s"), l1)
                for kvh in range(2):
                    for b in range(DEC_B):
                        pe.transpose(ps[:, 4 + 2 * kvh + b // 4, (b % 4) * P:(b % 4 + 1) * P],
                                     prob_s[:, kvh, b * P:(b + 1) * P], c("ident"))
                for kvh in range(2):
                    mm = pe.transpose(ps[0:TS, 2, kvh * P:(kvh + 1) * P], prob_s[:, kvh, 1024:1056], c("ident"))
                mm.then_inc(E("probs_s_turned"), 1)
                yield from at("smp_pv")
                pe.wait_ge(E("probs_s_copied"), l1)
                for kvh in range(2):
                    r = slice(64 * kvh, 64 * kvh + 64)
                    pe.matmul(ps[r, 3, 0:P], vs[0:TS, 0, r], prob_nt[0:TS, kvh, :], start=True, stop=False,
                              skip_group_check=True)
                    for b in range(DEC_B):
                        cols = slice(DEC_T * b, DEC_T * b + DEC_T)
                        mm = pe.matmul(ps[r, 3, 0:P].rearrange("p (j n) -> p j n", j=4)[:, :, cols], v_hist[:, b, r],
                                       prob_st[:, kvh, b, :].rearrange("p (j n) -> p j n", j=4)[:, :, cols],
                                       start=False, stop=b == DEC_B - 1, skip_group_check=True)
                mm.then_inc(E("smp_pv"), 1)
                yield from at("decay_in")
                pe.wait_ge(E("lr_ready"), l1)
                pe.wait_ge(small_in, l1 * 48)
                for k in range(2):
                    mm = pe.matmul(ps[:, 4 + k, 0:T], w_a2[0:16, k * P:(k + 1) * P], lr[0:16, :], start=True, stop=True)
                mm.then_inc(E("decay_in"), 1)
                pe.wait_ge(E("smp_od"), l1)
                pe.wait_ge(E("z_gla"), l1)
                for h in range(4):
                    for a in range(2):
                        pe.transpose(ps[:, 6 + a, h * P:(h + 1) * P], z[:, A_V + h, a * P:(a + 1) * P], c("ident"))
                for h in range(4):
                    mm = pe.transpose(ps[0:TS, 2, h * P:(h + 1) * P], z[:, A_V + h, SEQ:T], c("ident"))
                mm.then_inc(E("v_turned"), 1)
                yield from at("att_in")
                pe.wait_ge(E("v_copied"), l1)
                pe.wait_ge(E("k_last_done"), l1)
                for a in range(2):
                    for k in range(2):
                        pe.transpose(ps[:, 6, (2 * a + k) * P:(2 * a + k + 1) * P], z[:, A_K + k, a * P:(a + 1) * P],
                                     c("ident"))
                for k in range(2):
                    mm = pe.transpose(ps[0:TS, 7, k * P:(k + 1) * P], z[:, A_K + k, SEQ:T], c("ident"))
                mm.then_inc(E("k_turned"), 1)
                for par in range(2):
                    r = slice(64 * par, 64 * par + 64)
                    for hp in range(2):
                        for ch in range(NSEG):
                            o = slice(64 * (ch % 2), 64 * (ch % 2) + 64)
                            col = (hp * 2 + ch // 2) * 64
                            tok = slice(ch * 64, ch * 64 + 64)
                            pe.matmul(ps[o, 4 + par, col:col + 64], k_neg[r, hp, tok], qz[r, 2 * hp + par, tok],
                                      start=True, stop=True)
                        mm = pe.matmul(ps[0:TS, 4 + par, 256 + hp * TS:256 + hp * TS + TS], k_neg[r, hp, SEQ:T],
                                       qz[r, 2 * hp + par, SEQ:T], start=True, stop=True)
                mm.then_inc(E("att_in"), 1)
                yield from at("chunks")
                pe.wait_ge(E("att_done"), l1)
                pe.wait_ge(E("k_copied"), l1)
                for h in range(4):
                    for a in range(2):
                        mm = pe.matmul(ps[:, 2 + a, h * P:(h + 1) * P], v_tok[:, a, h * P:(h + 1) * P], attz[:, h, a, :],
                                       start=h == 0, stop=False, skip_group_check=True)
                mm.then_inc(E("chunk_out"), 1)
                for ch in range(NSEG):
                    a, rows = ch // 2, slice(64 * (ch % 2), 64 * (ch % 2) + 64)
                    for k in range(2):
                        mm = pe.matmul(ps[:, 4 + ch % 2, k * 256:k * 256 + 256], k_tok[rows, a, k * P:(k + 1) * P],
                                       v_tok[rows, a, k * 256:k * 256 + 256], start=True, stop=True)
                    mm.then_inc(E("update"), 1)
                    if ch >= 1:
                        pe.wait_ge(E("state_step"), l * NSEG + ch)
                        for k in range(2):
                            out = ps[:, 2 + a, :].rearrange("p (h i) -> p h i", h=4)
                            mm = pe.matmul(out[:, 2 * k:2 * k + 2, 64 * (ch % 2):64 * (ch % 2) + 64], state[:, k, :],
                                           qz[:, 2 * k:2 * k + 2, ch * 64:ch * 64 + 64], start=False, stop=True,
                                           skip_group_check=True)
                        mm.then_inc(E("chunk_out"), 1)
                    if ch == 1:
                        yield
                yield from at("smp_old")
                pe.wait_ge(state_in, l1 * 16)
                pe.wait_ge(E("q_own_done"), l1)
                for k in range(2):
                    for b in range(DEC_B):
                        mm = pe.matmul(ps[64 * k:64 * k + 64, 7, 0:P], q_own[:, b, 64 * k:64 * k + 64], s_smp[:, b, k, :],
                                       start=b == 0, stop=b == DEC_B - 1)
                mm.then_inc(E("smp_old"), 1)
                yield from at("smp_out")
                for h in range(4):
                    pe.matmul(ps[:, 6, h * TS:h * TS + TS], v_tok_s[0:TS, h * P:(h + 1) * P], att_s[0:TS, h, :],
                              start=h == 0, stop=False, skip_group_check=True)
                pe.wait_ge(E("old_out"), l1)
                pe.matmul(ps[:, 6, 0:P], old_out, c("ident"), start=False, stop=True, skip_group_check=True)\
                    .then_inc(E("smp_out"), 1)
                yield from at("cv_mean")
                pe.wait_ge(E("cv_added"), l1)
                sum_of(7, added, "cv_mean")
                yield from at("smp_update")
                pe.wait_ge(E("k_own_done"), l1)
                pe.wait_ge(E("state_done"), l1)
                for b in range(DEC_B):
                    if b and b % 2 == 0:
                        yield
                    if b >= 2:
                        pe.wait_ge(E("smp_added"), l * DEC_B + b - 1)
                    for k in range(2):
                        mm = pe.matmul(ps[:, 4 + b % 2, k * 256:k * 256 + 256], k_own[0:TS, b, k * P:(k + 1) * P],
                                       v_tok_s[0:TS, k * 256:k * 256 + 256], start=True, stop=True)
                    mm.then_inc(E("smp_update"), 1)
                yield from at("gla_sums")
                pe.wait_ge(E("gla_sq"), l1)
                pe.wait_ge(E("cv_centred"), l1)
                for h in range(4):
                    mm = pe.matmul(ps[:, (2, 3, 6, 7)[h], 0:T], c("ones"), z[:, A_V + h, :], start=True, stop=True)
                mm.then_inc(E("gla_sums"), 1)
                yield from at("cv_var")
                pe.wait_ge(E("cv_sq_added"), l1)
                sum_of(5, added, "cv_var")
                yield from at("gm_mean")
                pe.wait_ge(E("gm_added"), l1)
                sum_of(4, added, "gm_mean")
                yield from at("gm_var")
                pe.wait_ge(E("gm_sq_added"), l1)
                sum_of(5, added, "gm_var")
                yield from at("gv_turned")
                pe.wait_ge(E("gv_done"), l1)
                for g in range(4):
                    for a in range(2):
                        pe.transpose(ps[:, 4 + a, g * P:(g + 1) * P], z[:, B_V + g, a * P:(a + 1) * P], c("ident"))
                    mm = pe.transpose(ps[0:TS, 6, g * P:(g + 1) * P], z[:, B_V + g, SEQ:T], c("ident"))
                mm.then_inc(E("gv_turned"), 1)
                pe.wait_ge(E("w_sp_masked"), l1)
                for g in range(4):
                    mm = pe.matmul(ps[0:TS, 7, g * DEC_T:g * DEC_T + DEC_T], c("rep", TS)[0:P], w_sp[:, g, 0:DEC_T],
                                   start=True, stop=True)
                mm.then_inc(E("corner"), 1)
                yield from at("mixed")
                pe.wait_ge(E("gv_copied"), l1)
                pe.wait_ge(E("w_bd_done"), l1)
                for g in range(4):
                    for a in range(2):
                        pe.matmul(ps[:, 4 + a, g * P:(g + 1) * P], gv_tok[:, a, g * P:(g + 1) * P], w_sp[:, g, :],
                                  start=True, stop=True)
                    mm = pe.matmul(ps[:, 7, g * TS:g * TS + TS], gv_tok_s[0:TS, g * P:(g + 1) * P], w_bd[0:TS, g, :],
                                   start=True, stop=True)
                mm.then_inc(E("mixed"), 1)

            with pe.Fori(0, DEPTH) as l:
                l1 = pe.snap(l + 1)
                mix = mixers(l, l1)
                for b, (t, u0, n) in enumerate(z_blocks()):
                    wait_lo(pe, l, Z0 + b)
                    if u0 == 0:
                        bank_wait(l, TZ + t)
                    for u in range(n):
                        if b == 0:
                            pe.wait_ge(xl_done, x_part_at(l, u))
                        mm = split_mm(ps[:, t % 2, 0:T], b % RING, u, x_hi[:, u0 + u, :], x_lo[:, u0 + u, :],
                                      u0 + u == 0, u0 + u == KC - 1)
                    mm.then_inc(blocks_done, 1)
                    place[0] = b
                    next(mix, None)
                for t in range(4 * KC):
                    wait_lo(pe, l, G0 + t)
                    bank_wait(l, TG + t)
                    for u in range(KC):
                        mm = split_mm(ps[:, t % 2, 0:T], t % RING, u, x_hi[:, u, :], x_lo[:, u, :], u == 0, u == KC - 1)
                    mm.then_inc(blocks_done, 1)
                    place[0] = G0 + t
                    next(mix, None)
                for b in range(2 * KC):
                    i = b // 4
                    wait_lo(pe, l, BR0 + b)
                    for d in range(2):
                        t = 2 * b + d
                        bank_wait(l, TB + t)
                        for u in range(4):
                            if t % 8 == 0:
                                pe.wait_ge(xl_done, x_part_at(l, KC + 4 * i + u))
                            rh, rl = branch_part(4 * i + u)
                            mm = split_mm(ps[:, t % 4, 0:T], b % RING, 4 * d + u, rh, rl, u == 0, u == 3)
                    mm.then_inc(blocks_done, 1)
                    place[0] = BR0 + b
                    next(mix, None)
                for _ in mix:
                    pass
                for t in range(KC):
                    wait_lo(pe, l, O0 + t)
                    bank_wait(l, TO + t)
                    for u in range(KC):
                        if t == 0:
                            pe.wait_ge(xl_done, x_part_at(l, 3 * KC + u))
                        mm = split_mm(ps[:, t % 4, 0:T], t % RING, u, m_hi[:, u, :], m_lo[:, u, :], u == 0, u == KC - 1)
                    mm.then_inc(blocks_done, 1)
                for s in range(RING):
                    wait_lo(pe, l, U0 + s)
                    bank_wait(l, TU + s)
                    for u in range(KC):
                        if s == 0:
                            pe.wait_ge(xl_done, x_part_at(l, 4 * KC + u))
                        mm = split_mm(ps[:, s, 0:T], s, u, x_hi[:, u, :], x_lo[:, u, :], u == 0, u == KC - 1)
                    mm.then_inc(blocks_done, 1)
                    if s == 0:
                        pe.wait_ge(squares, l1 * (KC - 1))
                        sum_of(7, sq[:, 0, :], "n2_sums")
                with pe.Fori(1, 2 * HC // RING) as i:
                    n = pe.snap(i * RING)
                    lo_at = [pe.snap(lo_dve_at(l, U0) + n)]
                    bank_at = [pe.snap(bank_at_turn(l, TU) + i)]
                    for s in range(RING):
                        pe.wait_ge(lo_dve, lo_at[s])
                        pe.wait_ge(bank_free[s], bank_at[s])
                        for u in range(KC):
                            mm = split_mm(ps[:, s, 0:T], s, u, x_hi[:, u, :], x_lo[:, u, :], u == 0, u == KC - 1)
                            if s + 1 < RING and u == 2:
                                lo_at.append(pe.snap(lo_at[0] + (s + 1)))
                            if s + 1 < RING and u == 4:
                                bank_at.append(pe.snap(bank_at_turn(l, TU + s + 1) + i))
                        mm.then_inc(blocks_done, 1)
                for t in range(KC):
                    done = 0
                    for q, n in enumerate(DOWN_UNITS):
                        b = DN0 + 3 * t + q
                        wait_lo(pe, l, b)
                        if q == 0:
                            bank_wait(l, TD + t)
                        for u in range(n):
                            if t == 0:
                                pe.wait_ge(hid_lo, l * HC + (done + u + 1))
                            mm = split_mm(ps[:, t % 4, 0:T], b % RING, u, h_hi[:, done + u, :], h_lo[:, done + u, :],
                                          done + u == 0, done + u == HC - 1)
                        done += n
                        mm.then_inc(blocks_done, 1)

        @block.scalar
        def _(act):
            place = [0]
            at = steps_of(place)

            chain = [0]

            def link(ins, l):
                ins.then_inc(act_link, 1)
                chain[0] += 1
                act.wait_ge(act_link, l * ACT_LINKS + chain[0])

            def split(l, b, dyn=0, dyn_slot=0):
                s = b % RING
                act.wait_ge(raw_in[s], l * (16 * (BLOCKS // RING)) + 16 * (b // RING + 1) + dyn_slot)
                act.wait_ge(blocks_done, slot_free_at(l, b) + dyn)
                act.activation(w_hi[:, s, :], raw[:, s, :], ACT.Copy).then_inc(hi_done, 1)

            def drain(l, b, t, out):
                act.wait_ge(blocks_done, block_done_at(l, b))
                act.activation(out, ps[:, t % 2, 0:T], ACT.Copy).then_inc(bank_free[t % 2], 1)

            def rstd(l, out, sums, n, eps, event):
                for o, v in zip(out, sums):
                    ins = act.activation(o, v, ACT.Ln, scale=1.0 / n, bias=c(eps, 1))
                link(ins, l)
                for o in out:
                    ins = act.activation(o, o, ACT.Exp, scale=-0.5)
                ins.then_inc(E(event), 1)

            def gates(l, i):
                act.wait_ge(E("gates_scaled"), l * 4 + i + 1)
                for k in range(KC):
                    t = i * KC + k
                    ins = act.activation(gate[:, t, :], gate[:, t, :], ACT.Sigmoid, bias=p("b_gate", t))
                ins.then_inc(E("gates_done"), 1)

            def mixers(l, l1):
                yield from at("n1_rstd")
                act.wait_ge(const_in, 16)
                act.wait_ge(E("n1_sums"), l1)
                rstd(l, [rs[:, :]], [ps[:, 7, 0:T]], D_MODEL, "eps6", "n1_rstd")
                yield from at("c_gate")
                act.wait_ge(E("z_conv"), l1)
                act.activation(z[:, C_G:C_G + 4, :], z[:, C_G:C_G + 4, :], ACT.Sigmoid).then_inc(E("c_gate"), 1)
                yield from at("qk_sq")
                act.wait_ge(E("z_att"), l1)
                act.activation(sq5, z[:, D_Q:D_Q + 5, :], ACT.Square).then_inc(E("qk_sq"), 1)
                yield from at("qk_rstd")
                act.wait_ge(E("qk_sums"), l1)
                rstd(l, [r5], [ps[:, 2:7, 0:T]], HD, "eps6", "qk_rstd")
                yield from at("tok_copied")
                act.wait_ge(E("tok_turned"), l1)
                act.activation(vt[:, :, :].rearrange("p a n -> p (a n)"), ps[:, 7, 0:2 * P], ACT.Copy)
                act.activation(vs[0:TS, :, :].rearrange("p a n -> p (a n)"), ps[0:TS, 7, 2 * P:4 * P], ACT.Copy)\
                    .then_inc(E("tok_copied"), 1)
                act.activation(q_smp[:, :].rearrange("p (j t) -> p j t", j=4), z[:, D_Q:D_Q + 4, SEQ:T], ACT.Copy)\
                    .then_inc(E("q_smp"), 1)
                for blk, src, sums in ((0, prob0, "exp0"), (1, prob1, "exp1")):
                    yield from at(sums)
                    act.wait_ge(E(f"shift{blk}"), l1)
                    for h in range(8):
                        ins = act.activation(src[:, h, :], src[:, h, :], ACT.Exp, bias=small[:, 1, 8 * blk + h:8 * blk + h + 1],
                                             accum_out=small[:, 3, 8 * blk + h:8 * blk + h + 1])
                    ins = act.activation(small[:, 2, 8 * blk:8 * blk + 8], small[:, 2, 8 * blk:8 * blk + 8], ACT.Exp)
                    ins.then_inc(E(sums), 1)
                yield from at("probs_copied")
                act.wait_ge(E("probs0_turned"), l1)
                act.activation(prob0_t, ps[:, 2:4, :], ACT.Copy)
                act.wait_ge(E("probs1_turned"), l1)
                act.activation(prob_t[:, 1024:3072], ps[:, 4:8, :], ACT.Copy).then_inc(E("probs1_copied"), 1)
                yield from at("prompt_od")
                act.wait_ge(E("prompt_pv"), l1)
                act.activation(z[:, D_Q:D_Q + 4, 0:P], ps[:, 2, :].rearrange("p (j q) -> p j q", j=4), ACT.Copy)
                act.activation(z[:, D_Q:D_Q + 4, P:SEQ], ps[:, 3, :].rearrange("p (j q) -> p j q", j=4), ACT.Copy)\
                    .then_inc(E("prompt_od"), 1)
                yield from at("exp_s")
                act.wait_ge(E("shift_s"), l1)
                for kvh in range(2):
                    act.activation(prob_s[:, kvh, :], prob_s[:, kvh, :], ACT.Exp, bias=small[:, 1, 16 + kvh:17 + kvh],
                                   accum_out=small[:, 3, 16 + kvh:17 + kvh])
                act.activation(small[:, 2, 16:18], small[:, 2, 16:18], ACT.Exp).then_inc(E("exp_s"), 1)
                yield from at("probs_s_copied")
                act.wait_ge(E("probs_s_turned"), l1)
                act.activation(prob_t[:, 0:2048], ps[:, 4:8, :], ACT.Copy)
                act.activation(prob_t[0:TS, 2048:2048 + 2 * P], ps[0:TS, 2, 0:2 * P], ACT.Copy)\
                    .then_inc(E("probs_s_copied"), 1)
                yield from at("smp_od")
                act.wait_ge(E("smp_pv"), l1)
                act.activation(z[:, D_Q:D_Q + 4, SEQ:T], ps[:, 3, 0:P].rearrange("p (j q) -> p j q", j=4), ACT.Copy)\
                    .then_inc(E("smp_od"), 1)
                act.dma_start(kv[:, :], dram["state"][bass.ds(l, 1)].rearrange("a p n -> (a p) n")).then_inc(state_in, 16)
                yield from at("decay_log")
                act.wait_ge(E("decay_in"), l1)
                for k in range(2):
                    ins = act.activation(e_last[:, k, :], ps[:, 4 + k, 0:T], ACT.Identity, bias=p("b_alpha", k))
                ins.then_inc(E("decay_y"), 1)
                act.wait_ge(E("decay_y"), l1)
                link(act.activation(e_pos, e_last, ACT.Abs), l)
                link(act.activation(e_pos, e_pos, ACT.Exp, scale=-1.0), l)
                act.activation(e_pos, e_pos, ACT.Ln, bias=1.0).then_inc(E("decay_log"), 1)
                yield from at("v_copied")
                act.wait_ge(E("v_turned"), l1)
                act.activation(v_tok, ps[:, 6:8, :], ACT.Copy)
                act.activation(v_tok_s[0:TS, :], ps[0:TS, 2, :], ACT.Copy).then_inc(E("v_copied"), 1)
                yield from at("decay_exp")
                act.wait_ge(E("decay_sum"), l1)
                act.activation(e_pos, bcum, ACT.Exp, scale=1.0 / 16).then_inc(E("e_pos_done"), 1)
                act.activation(k_neg, bcum, ACT.Exp, scale=-1.0 / 16).then_inc(E("e_neg_done"), 1)
                act.wait_ge(E("last_diff"), l1)
                act.activation(e_last, e_last, ACT.Exp, scale=1.0 / 16).then_inc(E("e_last_done"), 1)
                yield from at("k_copied")
                act.wait_ge(E("k_turned"), l1)
                act.activation(k_tok, ps[:, 6, :].rearrange("p (a n) -> p a n", a=2), ACT.Copy)
                act.activation(k_tok_s[0:TS, :], ps[0:TS, 7, 0:2 * P], ACT.Copy).then_inc(E("k_copied"), 1)
                yield from at("gelu")
                act.wait_ge(E("z_gmlp"), l1)
                act.activation(z[:, B_V:B_V + 4, :], z[:, B_V:B_V + 4, :], ACT.Gelu).then_inc(E("v_gelu"), 1)
                act.activation(z[:, B_U:B_U + 4, :], z[:, B_U:B_U + 4, :], ACT.Gelu).then_inc(E("u_gelu"), 1)
                yield from at("old_out")
                act.wait_ge(E("smp_old"), l1)
                act.activation(old_out, ps[:, 7, 0:P], ACT.Copy).then_inc(E("old_out"), 1)
                yield from at("gla_o")
                for a in range(2):
                    act.wait_ge(E("chunk_out"), l * NSEG + 2 * a + 2)
                    act.activation(gla_o[:, :, a * P:(a + 1) * P], ps[:, 2 + a, :].rearrange("p (h i) -> p h i", h=4), ACT.Copy)
                act.wait_ge(E("smp_out"), l1)
                link(act.activation(gla_o[:, :, SEQ:T], ps[:, 6, 0:4 * TS].rearrange("p (h i) -> p h i", h=4), ACT.Copy), l)
                act.activation(z[:, A_V:A_V + 4, :], gla_o, ACT.Square).then_inc(E("gla_sq"), 1)
                yield from at("cv_sq")
                act.wait_ge(E("cv_centred"), l1)
                act.activation(c_sq, z[:, C_A:C_A + 4, :], ACT.Square).then_inc(E("cv_sq"), 1)
                yield from at("gla_rstd")
                act.wait_ge(E("gla_sums"), l1)
                act.wait_ge(E("cv_var"), l1)
                for h in range(2):
                    act.activation(g_tmp[:, 2 * h:2 * h + 2, :], ps[:, 2 + 4 * h:4 + 4 * h, 0:T], ACT.Ln, scale=1.0 / P,
                                   bias=c("eps6", 1))
                link(act.activation(rs_m[:, :], ps[:, 5, 0:T], ACT.Ln, scale=1.0 / 512, bias=c("eps5", 1)), l)
                act.activation(g_tmp, g_tmp, ACT.Exp, scale=-0.5).then_inc(E("gla_rstd"), 1)
                act.activation(rs_m[:, :], rs_m[:, :], ACT.Exp, scale=-0.5).then_inc(E("cv_rstd"), 1)
                yield from at("r_silu")
                act.activation(z[:, A_R:A_R + 4, :], z[:, A_R:A_R + 4, :], ACT.Silu).then_inc(E("r_silu"), 1)
                yield from at("c_silu")
                act.wait_ge(E("cv_scaled"), l1)
                for k in range(4):
                    ins = act.activation(z[:, C_A + k, :], z[:, C_A + k, :], ACT.Silu, scale=p("conv_g", k),
                                         bias=p("conv_lb", k))
                ins.then_inc(E("c_out"), 1)
                yield from at("a_parts")
                act.wait_ge(E("a_out"), l1)
                for k in range(4):
                    branch_input(l, k, z[:, A_R + k, :])
                yield from at("gates0")
                gates(l, 0)
                yield from at("gm_sq")
                act.wait_ge(E("gm_centred"), l1)
                act.activation(g_sq, z[:, B_V:B_V + 4, :], ACT.Square).then_inc(E("gm_sq"), 1)
                yield from at("gates1")
                gates(l, 1)
                yield from at("gv_done")
                act.wait_ge(E("gm_var"), l1)
                rstd(l, [rs_m[:, :]], [ps[:, 5, 0:T]], 512, "eps5", "gm_rstd")
                act.wait_ge(E("gm_scaled"), l1)
                for k in range(4):
                    ins = act.activation(z[:, B_V + k, :], z[:, B_V + k, :], ACT.Identity, scale=p("gmlp_g", k),
                                         bias=p("gmlp_b", k))
                ins.then_inc(E("gv_done"), 1)
                yield from at("gv_copied")
                act.wait_ge(E("gv_turned"), l1)
                act.activation(gv_tok, ps[:, 4:6, :], ACT.Copy)
                act.activation(gv_tok_s[0:TS, :], ps[0:TS, 6, :], ACT.Copy).then_inc(E("gv_copied"), 1)
                yield from at("gates2")
                gates(l, 2)
                yield from at("gates3")
                gates(l, 3)

            def merged_part(l, k):
                act.wait_ge(summed, l * (3 * KC) + (2 * KC + k + 1))
                act.activation(m_hi[:, k, :], gate[:, k, :], ACT.Copy).then_inc(xh_done, 1)

            def branch_input(l, k, src):
                act.activation(branch_part(k)[0], src, ACT.Copy).then_inc(xh_done, 1)

            def normed_part(l, which, k):
                act.activation(x_hi[:, k, :], x[:, k, :], ACT.Copy, scale=p(f"norm{which}", k)).then_inc(xh_done, 1)

            def square(k):
                act.activation(sq[:, k, :], x[:, k, :], ACT.Square).then_inc(sq_done, 1)

            act.dma_start(x[:, KC // 2:KC, :], x_half(1)).then_inc(x_in[1], 16)
            act.wait_ge(zeroed, 1)
            act.activation(vt[:, 0, 0:1], hist_p[:, 0, 0:1], ACT.Copy)
            act.wait_ge(x_in[0], 16)
            act.wait_ge(x_in[1], 16)
            act.dma_start(cst[:, :], dram["consts"]).then_inc(const_in, 16)
            with act.Fori(0, DEPTH) as l:
                chain[0] = 0
                l1 = act.snap(l + 1)
                split(l, 0)
                act.wait_ge(prm_in, l1 * 16)
                for k in range(KC):
                    if k == KC // 2:
                        split(l, 1)
                    bank = bank_of(TD + k)
                    act.wait_ge(bank_free[bank], l * PER_BANK[bank] + (turn_of(TD + k) + 2 - PER_BANK[bank]))
                    normed_part(l, 1, k)
                split(l, 2)
                mix = mixers(l, l1)
                done = None
                for b, (t, u0, n) in enumerate(z_blocks()):
                    split(l, b + 3)
                    if done is not None:
                        drain(l, Z0 + b - 1, TZ + done, z[:, done, :])
                    done = t if u0 + n == KC else None
                    place[0] = b
                    next(mix, None)
                for t in range(4 * KC):
                    split(l, G0 + t + 3)
                    if t == 0:
                        drain(l, G0 - 1, TZ + NZ - 1, z[:, NZ - 1, :])
                    else:
                        drain(l, G0 + t - 1, TG + t - 1, gate[:, t - 1, :])
                    place[0] = G0 + t
                    next(mix, None)
                drain(l, BR0 - 1, TB - 1, gate[:, 4 * KC - 1, :])
                for b in range(2 * KC):
                    split(l, BR0 + b + 3)
                    for step, i in SPLIT_STEPS.items():
                        if STEP[step] != BR0 + b:
                            continue
                        tile, event = BRANCH_IN[i]
                        act.wait_ge(E(event), l1)
                        if i == 3:
                            act.wait_ge(blocks_done, block_done_at(l, BR0 + 7))
                        for k in range(4):
                            branch_input(l, 4 * i + k, z[:, tile + k, :])
                    place[0] = BR0 + b
                    next(mix, None)
                    if b > 12:
                        for k in (2 * (b - 13), 2 * (b - 13) + 1):
                            merged_part(l, k)
                for k in (KC - 2, KC - 1):
                    merged_part(l, k)
                for t in range(KC):
                    split(l, O0 + t + 3)
                    if t:
                        wait_drained(act, l, TO + t - 1)
                        square(t - 1)
                        normed_part(l, 2, t - 1)
                act.wait_ge(stored, l1 * (16 * STORES_PER_LAYER))
                wait_drained(act, l, TO + KC - 1)
                normed_part(l, 2, KC - 1)
                square(KC - 1)
                act.wait_ge(E("n2_sums"), l1)
                rstd(l, [rs[:, :]], [ps[:, 7, 0:T]], D_MODEL, "eps6", "n2_rstd")
                act.wait_ge(E("n2_rstd"), l1)
                with act.Fori(0, 2 * HC // RING) as i:
                    n = act.snap(i * RING)
                    for s in range(RING):
                        if s % 2 == 0:
                            wait_drained(act, l, TU + s, i)
                            act.activation(gate_s[:, s // 2, :], gate_s[:, s // 2, :], ACT.Silu).then_inc(silu_done, 1)
                            split(l, U0 + s + 3, n, i * 16)
                            split(l, U0 + s + 4, n, i * 16)
                        else:
                            wait_drained(act, l, TU + s, i)
                            act.activation(h_hi[:, bass.ds(i * 2 + s // 2, 1), :], hidden[:, s // 2:s // 2 + 1, :], ACT.Copy)\
                                .then_inc(hid_hi, 1)
                for t in range(KC):
                    for b in range(DN0 + 3 * t + 3, min(DN0 + 3 * t + 6, BLOCKS)):
                        split(l, b)
                assert chain[0] == ACT_LINKS, chain[0]

        @block.vector
        def _(dve):
            chain = [0]
            place = [0]
            at = steps_of(place)

            def link(ins, l):
                ins.then_inc(dve_link, 1)
                chain[0] += 1
                dve.wait_ge(dve_link, l * DVE_LINKS + chain[0])

            def split(l, b, dyn=0):
                if b >= POOL_BLOCKS:
                    s = b % RING
                    dve.wait_ge(hi_done, l * BLOCKS + (b + 1) + dyn)
                    dve.tensor_tensor(w_lo[:, s, :], raw[:, s, :], w_hi[:, s, :].bitcast(f32), ALU.subtract)\
                        .then_inc(lo_dve, 1)

            def merged_part(l, k):
                dve.wait_ge(xh_done, x_part_at(l, 3 * KC + k))
                dve.tensor_tensor(m_lo[:, k, :], gate[:, k, :], m_hi[:, k, :].bitcast(f32), ALU.subtract).then_inc(xl_done, 1)

            def branch_input(l, k, src):
                hi, lo = branch_part(k)
                dve.wait_ge(xh_done, x_part_at(l, KC + k))
                dve.tensor_tensor(lo, src, hi.bitcast(f32), ALU.subtract).then_inc(xl_done, 1)

            def normed_part(l, which, count, k):
                dve.wait_ge(xh_done, x_part_at(l, count + k))
                dve.scalar_tensor_tensor(out=x_lo[:, k, :], in0=x[:, k, :], scalar=p(f"norm{which}", k),
                                         in1=x_hi[:, k, :].bitcast(f32), op0=ALU.mult, op1=ALU.subtract).then_inc(xl_done, 1)

            def bcast(ap, n):
                return ap.unsqueeze(1).to_broadcast([P, n, ap.shape[1]])

            def scale_bias(l, l1, first, last, event):
                dve.wait_ge(E("n1_rstd"), l1)
                for t in (last - 2, last - 1):
                    wait_drained(dve, l, TZ + t)
                v = z[:, first:last, :]
                link(dve.tensor_tensor(v, v, bcast(rs[:, :], last - first), ALU.mult), l)
                for t in range(first, last):
                    ins = dve.tensor_scalar(z[:, t, :], z[:, t, :], p("b_in", t), None, ALU.add)
                ins.then_inc(E(event), 1)
                dve.wait_ge(E(event), l1)

            def scale_gates(l, i):
                for t in (TG + i * KC + KC - 2, TG + i * KC + KC - 1):
                    wait_drained(dve, l, t)
                v = gate[:, i * KC:(i + 1) * KC, :]
                dve.tensor_tensor(v, v, bcast(rs[:, :], KC), ALU.mult).then_inc(E("gates_scaled"), 1)

            def conv(l, l1):
                scale_bias(l, l1, C_A, C_G + 4, "z_conv")
                dve.wait_ge(E("c_gate"), l1)
                dve.wait_ge(hist_in, l1 * 16)
                link(dve.tensor_tensor(hist_p[:, :, HIST:HIST + SEQ], z[:, C_A:C_A + 4, 0:SEQ], z[:, C_G:C_G + 4, 0:SEQ], ALU.mult), l)
                dve.tensor_tensor(hist_s[:, :, :, HIST:EXT], z[:, C_A:C_A + 4, SEQ:T].rearrange("p c (b t) -> p c b t", t=DEC_T),
                                  z[:, C_G:C_G + 4, SEQ:T].rearrange("p c (b t) -> p c b t", t=DEC_T), ALU.mult)\
                    .then_inc(E("conv_h"), 1)
                yield
                dve.wait_ge(E("conv_h"), l1)
                for k in range(4):
                    taps = p("conv_w", k * CONV_K, CONV_K)
                    link(dve.tensor_tensor(window.rearrange("p (b t k) -> p b t k", b=DEC_B, t=DEC_T), taps_of(k),
                                           taps.unsqueeze(1).unsqueeze(1).to_broadcast([P, DEC_B, DEC_T, CONV_K]), ALU.mult), l)
                    link(dve.tensor_reduce(z[:, C_A + k, SEQ:T], window.rearrange("p (n k) -> p n k", k=CONV_K), AX.X, ALU.add), l)
                    if k == 1:
                        yield
                for k in range(4):
                    ins = dve.tensor_scalar(z[:, C_A + k, SEQ:T], z[:, C_A + k, SEQ:T], p("conv_b", k), None, ALU.add)
                ins.then_inc(E("conv_samples"), 1)
                yield
                first = chain[0]
                for tap in range(CONV_K):
                    for k in range(4):
                        src = hist_p[:, k, tap:tap + SEQ]
                        acc = z[:, C_A + k, 0:SEQ]
                        w = p("conv_w", k * CONV_K + tap)
                        if tap:
                            dve.wait_ge(dve_link, l * DVE_LINKS + before[k])
                            ins = dve.scalar_tensor_tensor(out=acc, in0=src, scalar=w, in1=acc, op0=ALU.mult, op1=ALU.add)
                        else:
                            if k == 0:
                                before = [0] * 4
                            ins = dve.tensor_scalar(acc, src, w, p("conv_b", k), ALU.mult, ALU.add)
                        if tap == CONV_K - 1 and k == 3:
                            ins.then_inc(E("conv_done"), 1)
                        else:
                            ins.then_inc(dve_link, 1)
                            chain[0] += 1
                            before[k] = chain[0]
                        if k % 2 == 1:
                            yield

            def add_chunks(src, event):
                dve.tensor_reduce(added, src.rearrange("p c t -> p t c"), AX.X, ALU.add).then_inc(E(event), 1)

            def layer_norm(l, l1, tile, mean_bank, squared, name):
                t4 = z[:, tile:tile + 4, :]
                add_chunks(t4, f"{name}_added")
                yield
                dve.wait_ge(E(f"{name}_mean"), l1)
                dve.scalar_tensor_tensor(out=t4, in0=bcast(ps[:, mean_bank, 0:T], 4), scalar=-1.0 / 512, in1=t4,
                                         op0=ALU.mult, op1=ALU.add).then_inc(E(f"{name}_centred"), 1)
                yield
                dve.wait_ge(E(f"{name}_sq"), l1)
                add_chunks(squared, f"{name}_sq_added")
                yield
                dve.wait_ge(E(f"{name}_rstd"), l1)
                dve.tensor_tensor(t4, t4, bcast(rs_m[:, :], 4), ALU.mult).then_inc(E(f"{name}_scaled"), 1)

            def softmax_in(l, l1, cols, event):
                link(dve.tensor_tensor(small[:, 0, cols], small[:, 0, cols], p("sink", 0, 18)[:, cols], ALU.max), l)
                dve.tensor_scalar(small[:, 1, cols], small[:, 0, cols], -1.0, None, ALU.mult)
                dve.tensor_tensor(small[:, 2, cols], p("sink", 0, 18)[:, cols], small[:, 0, cols], ALU.subtract)\
                    .then_inc(E(event), 1)

            def softmax_out(l, l1, cols, probs, event):
                link(dve.tensor_tensor(small[:, 3, cols], small[:, 3, cols], small[:, 2, cols], ALU.add), l)
                link(dve.reciprocal(small[:, 4, cols], small[:, 3, cols]), l)
                n, m = probs.shape[1], probs.shape[2]
                dve.tensor_tensor(probs, probs, small[:, 4, cols].unsqueeze(2).to_broadcast([P, n, m]), ALU.mult)\
                    .then_inc(E(event), 1)

            def mixers(l, l1, conv_steps):
                scale_bias(l, l1, D_Q, D_V + 1, "z_att")
                dve.wait_ge(const_in, 16)
                yield
                dve.wait_ge(E("qk_rstd"), l1)
                dve.scalar_tensor_tensor(out=z[:, D_Q:D_Q + 4, :], in0=z[:, D_Q:D_Q + 4, :], scalar=p("q_g"), in1=r5[:, 0:4, :],
                                         op0=ALU.mult, op1=ALU.mult)
                dve.scalar_tensor_tensor(out=z[:, D_K, :], in0=z[:, D_K, :], scalar=p("k_g"), in1=r5[:, 4, :],
                                         op0=ALU.mult, op1=ALU.mult).then_inc(E("qk_normed"), 1)
                yield
                dve.wait_ge(E("qk_turned"), l1)
                link(dve.tensor_tensor(r5, ps[:, 2:7, 0:T], bcast(c("sin", T), 5), ALU.mult), l)
                dve.wait_ge(E("qk_normed"), l1)
                link(dve.tensor_tensor(z[:, D_Q:D_Q + 5, :], z[:, D_Q:D_Q + 5, :], bcast(c("cos", T), 5), ALU.mult), l)
                dve.tensor_tensor(z[:, D_Q:D_Q + 5, :], z[:, D_Q:D_Q + 5, :], r5, ALU.add).then_inc(E("qk_done"), 1)
                yield
                dve.wait_ge(E("scores0"), l1)
                link(dve.scalar_tensor_tensor(out=prob0, in0=ps[:, 2:4, :].rearrange("p a (h k) -> p (a h) k", k=P),
                                              scalar=HD ** -0.5, in1=bcast(c("band", P, P), 8), op0=ALU.mult, op1=ALU.add), l)
                link(dve.tensor_reduce(small[:, 0, 0:8], prob0, AX.X, ALU.max), l)
                softmax_in(l, l1, slice(0, 8), "shift0")
                yield
                dve.wait_ge(E("scores1"), l1)
                link(dve.scalar_tensor_tensor(out=prob1, in0=ps[:, 4:8, :].rearrange("p a (h k) -> p (a h) k", k=2 * P),
                                              scalar=HD ** -0.5, in1=bcast(c("band", 2 * P), 8), op0=ALU.mult, op1=ALU.add), l)
                link(dve.tensor_reduce(small[:, 0, 8:16], prob1, AX.X, ALU.max), l)
                softmax_in(l, l1, slice(8, 16), "shift1")
                yield
                dve.wait_ge(E("exp0"), l1)
                softmax_out(l, l1, slice(0, 8), prob0, "probs0")
                yield
                dve.wait_ge(E("exp1"), l1)
                softmax_out(l, l1, slice(8, 16), prob1, "probs1")
                yield
                yield
                dve.wait_ge(E("probs1_turned"), l1)
                dve.wait_ge(E("smp_hist"), l1)
                own = c("own", DEC_B).unsqueeze(2).to_broadcast([P, DEC_B, P])
                for kvh in range(2):
                    ins = dve.scalar_tensor_tensor(
                        out=prob_s[:, kvh, 0:1024].rearrange("p (b s) -> p b s", b=DEC_B),
                        in0=ps[:, 4 + 2 * kvh:6 + 2 * kvh, :].rearrange("p a (b s) -> p (a b) s", s=P),
                        scalar=HD ** -0.5, in1=own, op0=ALU.mult, op1=ALU.add)
                link(ins, l)
                for kvh in range(2):
                    v = prob_s[:, kvh, 0:1024].rearrange("p (b s) -> p b s", b=DEC_B)
                    dve.tensor_tensor(v, v, bcast(c("later"), DEC_B), ALU.add)
                yield
                dve.wait_ge(E("smp_new"), l1)
                link(dve.scalar_tensor_tensor(out=prob_s[:, :, 1024:1056], in0=ps[:, 2:4, 0:TS], scalar=HD ** -0.5,
                                              in1=bcast(c("new", TS), 2), op0=ALU.mult, op1=ALU.add), l)
                link(dve.tensor_reduce(small[:, 0, 16:18], prob_s, AX.X, ALU.max), l)
                softmax_in(l, l1, slice(16, 18), "shift_s")
                yield
                dve.wait_ge(E("exp_s"), l1)
                softmax_out(l, l1, slice(16, 18), prob_s, "probs_s")
                yield
                yield
                scale_bias(l, l1, A_Q, A_R + 4, "z_gla")
                yield
                dve.wait_ge(E("decay_y"), l1)
                link(dve.tensor_scalar(bcum, e_last, 0.0, None, ALU.min), l)
                dve.wait_ge(E("decay_log"), l1)
                link(dve.tensor_tensor(bcum, bcum, e_pos, ALU.subtract), l)
                for k in range(2):
                    ins = dve.tensor_tensor_scan(e_last[:, k, :], c("seg", T), bcum[:, k, :], 0.0, ALU.mult, ALU.add)
                link(ins, l)
                dve.tensor_copy(bcum, e_last).then_inc(E("decay_sum"), 1)
                dve.wait_ge(E("decay_sum"), l1)
                for k in range(2):
                    v, w = e_last[:, k, 0:SEQ].rearrange("p (n i) -> p n i", i=64), bcum[:, k, 0:SEQ].rearrange("p (n i) -> p n i", i=64)
                    dve.tensor_tensor(v, w[:, :, 63:64].to_broadcast([P, NSEG, 64]), w, ALU.subtract)
                    v, w = e_last[:, k, SEQ:T].rearrange("p (n i) -> p n i", i=DEC_T), bcum[:, k, SEQ:T].rearrange("p (n i) -> p n i", i=DEC_T)
                    ins = dve.tensor_tensor(v, w[:, :, DEC_T - 1:DEC_T].to_broadcast([P, DEC_B, DEC_T]), w, ALU.subtract)
                ins.then_inc(E("last_diff"), 1)
                yield
                dve.wait_ge(E("e_pos_done"), l1)
                for par in range(2):
                    r = slice(64 * par, 64 * par + 64)
                    dve.scalar_tensor_tensor(out=qz[r, par:4:2, :], in0=z[r, A_Q:A_Q + 2, :], scalar=64 ** -0.5, in1=e_pos[r, :, :],
                                             op0=ALU.mult, op1=ALU.mult)
                dve.wait_ge(E("e_neg_done"), l1)
                dve.tensor_tensor(k_neg, z[:, A_K:A_K + 2, :], k_neg, ALU.mult).then_inc(E("k_neg_done"), 1)
                dve.wait_ge(E("e_last_done"), l1)
                dve.wait_ge(E("k_neg_done"), l1)
                dve.tensor_tensor(z[:, A_K:A_K + 2, :], z[:, A_K:A_K + 2, :], e_last, ALU.mult).then_inc(E("k_last_done"), 1)
                yield
                scale_bias(l, l1, B_U, B_V + 4, "z_gmlp")
                dve.wait_ge(E("att_in"), l1)
                for par in range(2):
                    for odd in range(2):
                        r = slice(64 * odd, 64 * odd + 64)
                        for hp in range(2):
                            dve.tensor_tensor(attz[r, 2 * hp + par, :, 64 * odd:64 * odd + 64],
                                              ps[r, 4 + par, hp * P:(hp + 1) * P].rearrange("p (a i) -> p a i", a=2),
                                              c("gla", 64)[r].unsqueeze(1).to_broadcast([64, 2, 64]), ALU.mult)
                    ins = dve.tensor_tensor(att_s[0:TS, par:4:2, :], ps[0:TS, 4 + par, 256:256 + 2 * TS].rearrange("p (h i) -> p h i", h=2),
                                            c("gla_s", TS)[0:TS].unsqueeze(1).to_broadcast([TS, 2, TS]), ALU.mult)
                ins.then_inc(E("att_done"), 1)
                dve.wait_ge(E("k_copied"), l1)
                dve.tensor_tensor(k_own[0:TS, :, :], k_tok_s[0:TS].unsqueeze(1).to_broadcast([TS, DEC_B, 2 * P]),
                                  c("of_b", DEC_B)[0:TS].unsqueeze(2).to_broadcast([TS, DEC_B, 2 * P]), ALU.mult)\
                    .then_inc(E("k_own_done"), 1)
                link(dve.memset(q_own, 0.0), l)
                dve.tensor_copy(own_columns(), qz[:, :, SEQ:T].rearrange("p h (b t) -> p h b t", t=DEC_T))\
                    .then_inc(E("q_own_done"), 1)
                yield
                for ch in range(NSEG):
                    dve.wait_ge(E("update"), l * NSEG + ch + 1)
                    if ch >= 1:
                        dve.wait_ge(E("chunk_out"), l * NSEG + ch + 1)
                    for k in range(2):
                        for par in range(2):
                            r = slice(64 * par, 64 * par + 64)
                            u = ps[r, 4 + ch % 2, k * 256 + par * P:k * 256 + par * P + P]
                            if ch == 0:
                                ins = dve.tensor_copy(state[r, k, :], u)
                            else:
                                ins = dve.scalar_tensor_tensor(out=state[r, k, :], in0=state[r, k, :],
                                                               scalar=e_pos[r, k, ch * 64 + 63:ch * 64 + 64], in1=u,
                                                               op0=ALU.mult, op1=ALU.add)
                    ins.then_inc(E("state_done") if ch == NSEG - 1 else E("state_step"), 1)
                    if ch < NSEG - 1:
                        dve.wait_ge(E("state_step"), l * NSEG + ch + 1)
                    yield
                for _ in conv_steps:
                    pass
                dve.wait_ge(E("conv_done"), l1)
                cv = layer_norm(l, l1, C_A, 7, c_sq, "cv")
                next(cv)
                dve.wait_ge(E("state_done"), l1)
                dve.nop().then_inc(E("state_step"), 1)
                dve.wait_ge(E("smp_old"), l1)
                last = e_pos[:, :, SEQ:T].rearrange("p a (b t) -> p b a t", t=DEC_T)[:, :, :, DEC_T - 1:DEC_T]
                for k in range(2):
                    ins = dve.tensor_tensor(s_smp[:, :, k, :], s_smp[:, :, k, :], last[:, :, k, :].to_broadcast([P, DEC_B, P]), ALU.mult)
                link(ins, l)
                next(cv)
                for b in range(DEC_B):
                    dve.wait_ge(E("smp_update"), l * DEC_B + b + 1)
                    for par in range(2):
                        r = slice(64 * par, 64 * par + 64)
                        u = ps[r, 4 + b % 2, :].rearrange("p (k n) -> p k n", k=2)[:, :, par * P:par * P + P]
                        ins = dve.tensor_tensor(s_smp[r, b, :, :], s_smp[r, b, :, :], u, ALU.add)
                    ins.then_inc(E("smp_added"), 1)
                    if b % 2:
                        yield
                dve.wait_ge(E("smp_added"), l * DEC_B + DEC_B)
                dve.nop().then_inc(E("state_s_done"), 1)
                next(cv)
                scale_gates(l, 0)
                dve.wait_ge(E("gla_rstd"), l1)
                link(dve.scalar_tensor_tensor(out=g_tmp, in0=gla_o, scalar=p("gla_g"), in1=g_tmp, op0=ALU.mult, op1=ALU.mult), l)
                dve.wait_ge(E("r_silu"), l1)
                dve.tensor_tensor(z[:, A_R:A_R + 4, :], z[:, A_R:A_R + 4, :], g_tmp, ALU.mult).then_inc(E("a_out"), 1)
                next(cv, None)
                for k in range(4):
                    branch_input(l, k, z[:, A_R + k, :])
                yield
                scale_gates(l, 1)

            def gmlp(l, l1):
                yield from at("gm_add")
                dve.wait_ge(E("v_gelu"), l1)
                norm = layer_norm(l, l1, B_V, 4, g_sq, "gm")
                next(norm)
                yield from at("gm_centre")
                next(norm)
                yield from at("gm_add2")
                next(norm)
                yield from at("gm_scale")
                next(norm, None)
                yield from at("w_bd")
                dve.wait_ge(E("corner"), l1)
                dve.tensor_tensor(w_bd[0:TS, :, :].rearrange("p g (b t) -> p g b t", t=DEC_T),
                                  ps[0:TS, 7, 0:4 * DEC_T].rearrange("p (g t) -> p g t", g=4).unsqueeze(2).to_broadcast([TS, 4, DEC_B, DEC_T]),
                                  c("of_b", DEC_B)[0:TS].unsqueeze(1).unsqueeze(3).to_broadcast([TS, 4, DEC_B, DEC_T]), ALU.mult)\
                    .then_inc(E("w_bd_done"), 1)
                yield from at("b_out")
                dve.wait_ge(E("mixed"), l1)
                dve.wait_ge(small_in, l1 * 48)
                for a in range(2):
                    ins = dve.tensor_tensor(g_tmp[:, :, a * P:(a + 1) * P], ps[:, 4 + a, :].rearrange("p (g t) -> p g t", g=4), b_sp[:, :, :], ALU.add)
                for g in range(4):
                    ins = dve.tensor_tensor(g_tmp[:, g, SEQ:T].rearrange("p (b t) -> p b t", t=DEC_T),
                                            ps[:, 7, g * TS:g * TS + TS].rearrange("p (b t) -> p b t", t=DEC_T),
                                            bcast(b_sp[:, g, 0:DEC_T], DEC_B), ALU.add)
                link(ins, l)
                dve.wait_ge(E("u_gelu"), l1)
                dve.tensor_tensor(z[:, B_U:B_U + 4, :], z[:, B_U:B_U + 4, :], g_tmp, ALU.mult).then_inc(E("b_out"), 1)

            dve.nop().then_inc(lo_dve, RING)
            dve.nop().then_inc(blocks_done, RING)
            for k in range(4):
                dve.nop().then_inc(bank_free[k], 1)
            dve.memset(hist_p[:, :, 0:HIST], 0.0).then_inc(zeroed, 1)
            dve.memset(qz[:, :, :], 0.0)
            dve.memset(attz[:, :, :, :], 0.0).then_inc(zeroed, 1)
            dve.wait_ge(zeroed, 2)
            dve.wait_ge(x_in[0], 16)
            dve.wait_ge(x_in[1], 16)
            with dve.Fori(0, DEPTH) as l:
                chain[0] = 0
                l1 = dve.snap(l + 1)
                dve.wait_ge(prm_in, l1 * 16)
                for k in range(KC):
                    normed_part(l, 1, 0, k)
                dve.wait_ge(w_lr_in, l1 * 16)
                dve.tensor_tensor(w_lr[:, :, :], w_lr[:, :, :], p("norm1", 0, KC).unsqueeze(2).to_broadcast([P, KC, 16]), ALU.mult)\
                    .then_inc(E("w_lr_ready"), 1)
                link(dve.tensor_tensor(sq, x[:, :, :], x[:, :, :], ALU.mult), l)
                add_chunks(sq, "n1_added")
                dve.wait_ge(E("lr_sums"), l1)
                dve.wait_ge(E("n1_rstd"), l1)
                link(dve.tensor_tensor(lr[0:16, :], ps[0:16, 6, 0:T], rs[0:16, :], ALU.mult), l)
                dve.tensor_scalar(lr[0:16, :], lr[0:16, :], p("b_lr")[0:16], None, ALU.add).then_inc(E("lr_ready"), 1)
                conv_steps = conv(l, l1)
                mix = mixers(l, l1, conv_steps)
                for _ in range(CONV_AHEAD):
                    next(conv_steps, None)
                for _ in mix:
                    for _ in range(CONV_BETWEEN):
                        next(conv_steps, None)
                gm = gmlp(l, l1)
                place[0] = BR0 - 1
                next(gm, None)
                for b in range(2 * KC):
                    split(l, BR0 + b + 3)
                    dve.wait_ge(blocks_done, block_done_at(l, BR0 + b))
                    if b % 4 == 0:
                        dve.wait_ge(E("gates_done"), l * 4 + b // 4 + 1)
                    for t in (2 * b, 2 * b + 1):
                        dve.tensor_tensor(gate[:, t, :], ps[:, t % 4, 0:T], gate[:, t, :], ALU.mult).then_inc(bank_free[t % 4], 1)
                    for step, i in (("scale2", 2), ("scale3", 3)):
                        if STEP[step] == BR0 + b:
                            scale_gates(l, i)
                    place[0] = BR0 + b
                    next(gm, None)
                    for step, i in SPLIT_STEPS.items():
                        if STEP[step] != BR0 + b:
                            continue
                        tile, event = BRANCH_IN[i]
                        dve.wait_ge(E(event), l1)
                        for k in range(4):
                            branch_input(l, 4 * i + k, z[:, tile + k, :])
                    if b > 12:
                        for k in (2 * (b - 13), 2 * (b - 13) + 1):
                            merged_part(l, k)
                for k in (KC - 2, KC - 1):
                    merged_part(l, k)
                for t in range(KC):
                    split(l, O0 + t + 3)
                    dve.wait_ge(blocks_done, block_done_at(l, O0 + t))
                    dve.tensor_tensor(x[:, t, :], ps[:, t % 4, 0:T], x[:, t, :], ALU.add).then_inc(bank_free[t % 4], 1)
                    if t:
                        normed_part(l, 2, 4 * KC, t - 1)
                normed_part(l, 2, 4 * KC, KC - 1)
                dve.wait_ge(stored, l1 * (16 * STORES_PER_LAYER))
                dve.wait_ge(cached, l1 * 32)
                dve.wait_ge(xl_done, x_part_at(l, 5 * KC - 1))
                dve.nop().then_inc(E("layer_free"), 1)
                with dve.Fori(0, 2 * HC // RING) as i:
                    n = dve.snap(i * RING)
                    dve.wait_ge(E("n2_rstd"), l1)
                    for s in range(RING):
                        k = s // 2
                        dve.wait_ge(blocks_done, block_done_at(l, U0 + s) + n)
                        if s % 2 == 0:
                            dve.tensor_tensor(gate_s[:, k, :], ps[:, s, 0:T], rs[:, :], ALU.mult).then_inc(bank_free[s], 1)
                            split(l, U0 + s + 3, n)
                        else:
                            dve.wait_ge(gate_ready, l * HC + (k + 1) + i * 2)
                            dve.tensor_tensor(hidden[:, k, :], ps[:, s, 0:T], gate_s[:, k, :], ALU.mult).then_inc(bank_free[s], 1)
                            split(l, U0 + s + 3, n)
                            dve.wait_ge(hid_hi, l * HC + (k + 1) + i * 2)
                            o = bass.ds(i * 2 + k, 1)
                            dve.tensor_tensor(h_lo[:, o, :], hidden[:, k:k + 1, :], h_hi[:, o, :].bitcast(f32), ALU.subtract)\
                                .then_inc(hid_lo, 1)
                for t in range(KC):
                    for b in range(DN0 + 3 * t + 3, min(DN0 + 3 * t + 6, BLOCKS)):
                        split(l, b)
                    dve.wait_ge(blocks_done, block_done_at(l, DN0 + 3 * t + 2))
                    dve.tensor_tensor(x[:, t, :], ps[:, t % 4, 0:T], x[:, t, :], ALU.add).then_inc(bank_free[t % 4], 1)
                assert chain[0] == DVE_LINKS, chain[0]

        @block.gpsimd
        def _(pool):
            def add_squares(n):
                for k in range(1, KC):
                    pool.wait_ge(sq_done, n * KC + (k + 1))
                    if k >= 2:
                        pool.wait_ge(squares, n * (KC - 1) + (k - 1))
                    pool.tensor_tensor(sq[:, 0, :], sq[:, 0, :], sq[:, k, :], ALU.add).then_inc(squares, 1)

            def lo_part(l, b):
                s = b % RING
                pool.wait_ge(hi_done, l * BLOCKS + (b + 1))
                pool.tensor_tensor(w_lo[:, s, :], raw[:, s, :], w_hi[:, s, :].bitcast(f32), ALU.subtract).then_inc(lo_pool, 1)

            with pool.Fori(0, DEPTH) as l:
                l1 = pool.snap(l + 1)
                for b in range(POOL_BLOCKS):
                    lo_part(l, b)
                    if b == G0:
                        pool.wait_ge(small_in, l1 * 48)
                        pool.wait_ge(const_in, 16)
                        pool.tensor_tensor(w_sp[:, :, :], w_sp[:, :, :], c("upper").unsqueeze(1).to_broadcast([P, 4, P]),
                                           ALU.mult).then_inc(E("w_sp_masked"), 1)
                for i in range(1, 4):
                    for d in range(KC):
                        t = i * KC + d
                        wait_drained(pool, l, TB + t)
                        if i >= 2:
                            pool.wait_ge(summed, l * (3 * KC) + (i - 2) * KC + d + 1)
                        pool.tensor_tensor(gate[:, d, :], gate[:, d, :], gate[:, t, :], ALU.add).then_inc(summed, 1)
                add_squares(l)
                with pool.Fori(0, HC // 2) as i:
                    for k in range(2):
                        pool.wait_ge(silu_done, l * HC + (k + 1) + i * 2)
                        pool.tensor_tensor(gate_s[:, k, :], gate_s[:, k, :], rs[:, :], ALU.mult).then_inc(gate_ready, 1)


def k_slot(k):
    if KC <= k < 3 * KC:
        i, u = (k - KC) // 4, (k - KC) % 4
        return 4 * (i % 2) + u
    return k % KC


def constants():
    t = np.zeros((P, CONSTS), np.float32)

    def put(name, a):
        t[0:a.shape[0], CONST_AT[name]:CONST_AT[name] + a.shape[1]] = a

    i = np.arange(P)
    put("ones", np.ones((P, P)))
    put("heads", i[:, None] // HD == i[None, :] // HD)
    half, rope = HD // 8, HD // 4
    turn = np.zeros((P, P))
    for h in (0, HD):
        for k in range(half):
            turn[h + half + k, h + k] = -1.0
            turn[h + k, h + half + k] = 1.0
    put("turn", turn)
    put("ident", np.eye(P))
    put("upper", i[:, None] <= i[None, :])
    d = i[:, None] - (np.arange(2 * P)[None, :] - P)
    put("band", np.where((d >= 0) & (d < WIN), 0.0, NEG))
    row_b, row_t = (i % TS) // DEC_T, i % DEC_T
    s, b = np.arange(TS), np.arange(DEC_B)
    put("own", np.where(row_b[:, None] == b[None, :], 0.0, NEG))
    put("later", np.where(i[None, :] > row_t[:, None], 0.0, NEG))
    put("new", np.where((s[None, :] // DEC_T == row_b[:, None]) & (s[None, :] % DEC_T <= row_t[:, None]), 0.0, NEG))
    put("eps6", np.full((P, 1), 1e-6))
    put("eps5", np.full((P, 1), 1e-5))
    tok = np.arange(T)
    first = np.where(tok < SEQ, tok % 64 == 0, tok % DEC_T == 0)
    put("seg", np.repeat(1.0 - first[None, :], P, 0))
    pos = np.where(tok < SEQ, tok, PAST + (tok - SEQ) % DEC_T).astype(np.float32)
    inv = np.exp(np.float32(-math.log(500000.0)) * np.arange(half, dtype=np.float32) * np.float32(2.0 / rope))
    ang = (pos[None, :] * inv[:, None]).astype(np.float32)
    cos, sin = np.ones((P, T)), np.zeros((P, T))
    for h in (0, HD):
        for k in (0, half):
            cos[h + k:h + k + half], sin[h + k:h + k + half] = np.cos(ang), np.sin(ang)
    put("cos", cos)
    put("sin", sin)
    put("gla", (i[:, None] % 64) <= np.arange(64)[None, :])
    put("gla_s", (s[:, None] // DEC_T == s[None, :] // DEC_T) & (s[:, None] <= s[None, :]))
    put("of_b", s[:, None] // DEC_T == b[None, :])
    put("rep", np.arange(P)[:, None] == s[None, :] % DEC_T)
    return t


def kernel(**inputs):
    import concourse.bacc as bacc
    from concourse.bass_utils import run_bass_kernel_spmd

    a = {k: np.asarray(v) for k, v in inputs.items()}
    L = DEPTH

    def per_feature(v):
        return v.reshape(L, -1, P).transpose(0, 2, 1)

    def blocks(w):
        k, n = w.shape[1] // P, w.shape[2] // P
        return np.ascontiguousarray(w.reshape(L, k, P, n, P).transpose(0, 3, 2, 1, 4)).reshape(L * n, P, k * P)

    heads = np.arange(8).reshape(2, 4).T.reshape(-1)
    q_cols = (heads[:, None] * HD + np.arange(HD)[None, :]).reshape(-1)
    span = lambda at, n: np.arange(at, at + n)
    cols = np.concatenate([span(2576, 512), span(3088, 512), 3600 + q_cols, span(4112, 128), span(4240, 128),
                           span(0, 256), span(256, 256), span(512, 512), span(1024, 512), span(1552, 512),
                           span(2064, 512)])
    w_in, w_br = a["w_in"], a["w_branch"]
    w_br3 = w_br[:, 3][:, q_cols]
    w_b = np.concatenate([w_br[:, 0:3], w_br3[:, None]], 1)[:, list(ORDER)]
    w_b = w_b.reshape(L, 4, 4, P, 4, 2, P).transpose(0, 1, 4, 3, 5, 2, 6)
    up = a["w_gate_up"].reshape(L, D_MODEL, 2, HC, P).transpose(0, 1, 3, 2, 4).reshape(L, D_MODEL, 2 * FFN)
    sink = a["sinks"]
    sink_p = np.broadcast_to(sink[:, None, :], (L, P, 8))
    sink_s = np.repeat(sink.reshape(L, 2, 4).transpose(0, 2, 1), TS, 1)
    b_lr = np.zeros((L, P, 1), np.float32)
    b_lr[:, 0:16, 0] = a["b_in"][:, 1536:1552]
    params = np.concatenate([
        per_feature(a["b_in"][:, cols]), per_feature(a["b_gate"].reshape(L, 4, D_MODEL)[:, list(ORDER)].reshape(L, -1)), per_feature(a["norm1_g"]), per_feature(a["norm2_g"]),
        per_feature(a["b_alpha"]), per_feature(a["gla_norm_g"]), per_feature(a["gmlp_ln_g"]), per_feature(a["gmlp_ln_b"]),
        a["conv_w"].reshape(L, CONV_K, 4, P).transpose(0, 3, 2, 1).reshape(L, P, 4 * CONV_K), per_feature(a["conv_b"]),
        per_feature(a["conv_ln_g"]), per_feature(a["conv_ln_b"]),
        np.concatenate([a["q_norm_g"]] * 2, 1)[:, :, None], np.concatenate([a["k_norm_g"]] * 2, 1)[:, :, None],
        sink_p, sink_p, sink_s, b_lr], 2)
    xs = np.concatenate([a["x_prompt"].reshape(SEQ, D_MODEL), a["x_sample"].reshape(TS, D_MODEL)], 0)
    arrays = {
        "x": xs.reshape(T, KC, P).transpose(2, 1, 0).reshape(P, KC * T),
        "consts": constants(),
        "params": params,
        "w_lr": w_in[:, :, 1536:1552].reshape(L, KC, P, 16).transpose(0, 2, 1, 3).reshape(L, P, KC * 16),
        "w_z": blocks(w_in[:, :, cols]),
        "w_gate": blocks(a["w_gate"].reshape(L, D_MODEL, 4, D_MODEL)[:, :, list(ORDER)].reshape(L, D_MODEL, -1)),
        "w_branch": w_b.reshape(L * 16, P, 1024),
        "w_out": blocks(a["w_out"]),
        "w_up": blocks(up),
        "w_down": blocks(a["w_down"]),
        "w_a2": a["w_alpha2"],
        "w_sp": a["w_spatial"].transpose(0, 3, 1, 2).reshape(L, P, 4 * P),
        "b_sp": np.broadcast_to(a["b_spatial"].reshape(L, 1, 4 * P), (L, P, 4 * P)),
        "conv_hist": a["state_conv"].reshape(L, DEC_B, HIST, 4, P).transpose(0, 4, 3, 1, 2).reshape(L, P, -1),
        "k_hist": a["cache_swa_k"].reshape(L, DEC_B, WIN, P).transpose(0, 3, 1, 2).reshape(L, P, -1),
        "v_hist": a["cache_swa_v"].reshape(L, DEC_B, WIN, P).transpose(0, 2, 1, 3).reshape(L, P, -1),
        "cache_k": a["cache_swa_k"].reshape(L, DEC_B, WIN, P),
        "cache_v": a["cache_swa_v"].reshape(L, DEC_B, WIN, P),
        "state": a["state_gla"].reshape(L, DEC_B, 2, P, 128).transpose(0, 3, 1, 2, 4).reshape(L, P, -1),
    }
    arrays = {k: np.ascontiguousarray(v) for k, v in arrays.items()}
    outs = {
        "y": (P, KC * T), "gmlp_v": (L, P, 4 * TS), "gla_prompt": (L, P, 2 * P), "gla_sample": (L, P, 2048),
        "conv_prompt": (L, P, 4 * HIST), "conv_sample": (L, P, 4 * DEC_B * EXT), "k_prompt": (L, P, WIN),
        "v_prompt": (L, P, WIN), "k_sample": (L, DEC_B, WIN, P), "v_sample": (L, DEC_B, WIN, P)}
    nc = bacc.Bacc("TRN2", target_bir_lowering=False, num_devices=1, dynamic_dma_scratch_size=1024)
    dram = {}
    for name, v in arrays.items():
        dram[name] = nc.dram_tensor(f"in_{name}", v.shape, mybir.dt.from_np(v.dtype), kind="ExternalInput").ap()
    for name, shape in outs.items():
        dram[name] = nc.dram_tensor(f"out_{name}", shape, mybir.dt.float32, kind="ExternalOutput").ap()
    trunk_program(nc, dram)
    r = run_bass_kernel_spmd(nc, [{f"in_{k}": v for k, v in arrays.items()}], core_ids=[0]).results[0]

    y = r["out_y"].reshape(P, KC, T).transpose(2, 1, 0).reshape(T, D_MODEL)
    gla_p = r["out_gla_prompt"].reshape(L, P, 2, 128).transpose(0, 2, 1, 3).reshape(L, 1, 4, 64, 128)
    gla_s = r["out_gla_sample"].reshape(L, P, DEC_B, 2, 128).transpose(0, 2, 3, 1, 4).reshape(L, DEC_B, 4, 64, 128)
    conv_p = r["out_conv_prompt"].reshape(L, P, 4, HIST).transpose(0, 3, 2, 1).reshape(L, 1, HIST, CONV_W)
    conv_s = r["out_conv_sample"].reshape(L, P, 4, DEC_B, EXT)[..., DEC_T:].transpose(0, 3, 4, 2, 1)\
        .reshape(L, DEC_B, HIST, CONV_W)
    token_rows = lambda v: v.transpose(0, 2, 1).reshape(L, 1, WIN, 2, HD)
    gm = r["out_gmlp_v"].reshape(L, P, 4, DEC_B, DEC_T).transpose(0, 3, 4, 2, 1).reshape(L, DEC_B, DEC_T, 512)
    out = (y[0:SEQ].reshape(1, SEQ, D_MODEL), y[SEQ:T].reshape(DEC_B, DEC_T, D_MODEL), gla_p, gla_s, conv_p, conv_s,
           token_rows(r["out_k_prompt"]), token_rows(r["out_v_prompt"]), r["out_k_sample"].reshape(L, DEC_B, WIN, 2, HD),
           r["out_v_sample"].reshape(L, DEC_B, WIN, 2, HD), gm)
    return tuple(np.ascontiguousarray(o) for o in out)
```
